# Optimizing a Trainium2 kernel written in Bass

```python
import jax, jax.numpy as jnp
from jax import lax
import numpy as np

D_MODEL = 1024
BATCH = 1
SEQ = 2048
DEPTH = 1
DEC_BATCH = 8
DEC_SEQ = 1
PAST_LEN = 16384
PAGE_SIZE = 128

POOL_WIDTH = D_MODEL // 2
POOL_WINDOWS = (2, 4, 8, 16)
N_POOL_GROUPS = len(POOL_WINDOWS)
POOL_GROUP = POOL_WIDTH // N_POOL_GROUPS
POOL_BUF = max(POOL_WINDOWS) - 1
CONV_WIDTH = D_MODEL - POOL_WIDTH
CONV_K = 31
CONV_BUF = CONV_K - 1
D_MIX = POOL_WIDTH + CONV_WIDTH
D_IN = POOL_WIDTH + 2 * CONV_WIDTH
N_EXPERTS = 64
N_EXPERT_GROUPS = 8
TOPK_GROUPS = 4
TOP_K = 8
D_EXPERT = D_MODEL // 4
ROUTED_SCALE = 2.5
EXPERT_BLOCK = 128
EPS = 1e-6

kernel_name = "hybrid_pool_conformer_moe_adaln_step"

def rms_norm(x, g):
    xf = x.astype(jnp.float32)
    y = xf * lax.rsqrt(jnp.mean(xf * xf, -1, keepdims=True) + EPS)
    return (y * g.astype(jnp.float32)).astype(x.dtype)

def modulate(h, shift, scale):
    return h * (1.0 + scale[:, None, :]) + shift[:, None, :]

def multi_scale_pool(u, prev, prev_valid):
    L = u.shape[1]
    full = jnp.concatenate([prev, u], axis=1)
    ff = full.astype(jnp.float32)
    cs = jnp.concatenate([jnp.zeros_like(ff[:, :1]), jnp.cumsum(ff, axis=1)], axis=1)
    end = cs[:, POOL_BUF + 1:]
    t = jnp.arange(L)
    outs = []
    for g, w in enumerate(POOL_WINDOWS):
        sl = slice(g * POOL_GROUP, (g + 1) * POOL_GROUP)
        start = cs[:, POOL_BUF + 1 - w: POOL_BUF + 1 - w + L, sl]
        cnt = jnp.minimum(w, t + 1 + prev_valid).astype(jnp.float32)
        outs.append((end[..., sl] - start) / cnt[None, :, None])
    mean = jnp.concatenate(outs, axis=-1)
    d = (mean - u.astype(jnp.float32)).astype(u.dtype)
    return d, full[:, -POOL_BUF:]

def causal_depthwise_conv(a, prev, w_dw, b_dw):
    full = jnp.concatenate([prev, a], axis=1)
    y = lax.conv_general_dilated(full, w_dw[:, None, :].astype(full.dtype), window_strides=(1,),
                                 padding='VALID', dimension_numbers=('NWC', 'WIO', 'NWC'),
                                 feature_group_count=a.shape[-1])
    return y + b_dw, full[:, -CONV_BUF:]

def route(hf, w_router, b_router):
    T = hf.shape[0]
    s = jax.nn.sigmoid(hf.astype(jnp.float32) @ w_router.astype(jnp.float32))
    sel = s + b_router.astype(jnp.float32)
    per = N_EXPERTS // N_EXPERT_GROUPS
    gscore = lax.top_k(sel.reshape(T, N_EXPERT_GROUPS, per), 2)[0].sum(-1)
    _, gidx = lax.top_k(gscore, TOPK_GROUPS)
    gmask = jax.nn.one_hot(gidx, N_EXPERT_GROUPS, dtype=jnp.float32).sum(1) > 0
    sel_m = jnp.where(jnp.repeat(gmask, per, axis=1), sel, -jnp.inf)
    _, idx = lax.top_k(sel_m, TOP_K)
    w = jnp.take_along_axis(s, idx, axis=1)
    w = w / jnp.sum(w, -1, keepdims=True) * ROUTED_SCALE
    return idx, w

def routed_experts(hf, idx, wts, w_gate, w_up, w_down):
    T, D = hf.shape
    A = T * TOP_K
    flat_e = idx.reshape(-1)
    flat_t = jnp.repeat(jnp.arange(T, dtype=jnp.int32), TOP_K)
    flat_w = wts.reshape(-1)
    order = jnp.argsort(flat_e)
    e_s, t_s, w_s = flat_e[order], flat_t[order], flat_w[order]
    counts = jnp.bincount(flat_e, length=N_EXPERTS)
    pcounts = (counts + EXPERT_BLOCK - 1) // EXPERT_BLOCK * EXPERT_BLOCK
    pends = jnp.cumsum(pcounts)
    pstart = pends - pcounts
    start = jnp.cumsum(counts) - counts
    dest = pstart[e_s] + (jnp.arange(A) - start[e_s])
    n_blocks = (A + EXPERT_BLOCK - 1) // EXPERT_BLOCK + N_EXPERTS
    P = n_blocks * EXPERT_BLOCK
    tok = jnp.full((P,), T, jnp.int32).at[dest].set(t_s)
    gate = jnp.zeros((P,), hf.dtype).at[dest].set(w_s.astype(hf.dtype))
    block_e = jnp.minimum(jnp.searchsorted(pends, jnp.arange(n_blocks) * EXPERT_BLOCK, side='right'),
                          N_EXPERTS - 1)
    xpad = jnp.concatenate([hf, jnp.zeros((1, D), hf.dtype)], axis=0)

    def one_block(args):
        tok_b, gate_b, e = args
        xb = xpad[tok_b]
        hb = jax.nn.silu(xb @ w_gate[e]) * (xb @ w_up[e])
        return (hb @ w_down[e]) * gate_b[:, None]

    out = lax.map(one_block, (tok.reshape(n_blocks, EXPERT_BLOCK), gate.reshape(n_blocks, EXPERT_BLOCK), block_e))
    return jax.ops.segment_sum(out.reshape(P, D), tok, num_segments=T + 1)[:T]

def layer(x, c, pool_prev, conv_prev, prev_valid, w_ada, b_ada, g_mix, w_in, w_pool, pool_scale,
          w_dw, b_dw, ln_g, ln_b, w_out, g_ffn, w_router, b_router, w_gate, w_up, w_down,
          ws_gate, ws_up, ws_down):
    B, L, D = x.shape
    mod = jax.nn.silu(c) @ w_ada + b_ada
    sh1, sc1, g1, sh2, sc2, g2 = jnp.split(mod, 6, axis=-1)
    h = modulate(rms_norm(x, g_mix), sh1, sc1)
    z = h @ w_in
    u = z[..., :POOL_WIDTH]
    v = z[..., POOL_WIDTH:POOL_WIDTH + CONV_WIDTH]
    gt = z[..., POOL_WIDTH + CONV_WIDTH:]
    d, new_pool = multi_scale_pool(u, pool_prev, prev_valid)
    d = d.reshape(B, L, N_POOL_GROUPS, POOL_GROUP)
    pool_out = jnp.einsum('blgc,gcd->blgd', d, w_pool).reshape(B, L, POOL_WIDTH) * pool_scale
    a = v * jax.nn.sigmoid(gt)
    yc, new_conv = causal_depthwise_conv(a, conv_prev, w_dw, b_dw)
    yf = yc.astype(jnp.float32)
    mu = jnp.mean(yf, -1, keepdims=True)
    var = jnp.mean(jnp.square(yf - mu), -1, keepdims=True)
    yn = (yf - mu) * lax.rsqrt(var + EPS) * ln_g.astype(jnp.float32) + ln_b.astype(jnp.float32)
    conv_out = jax.nn.silu(yn).astype(x.dtype)
    mix = jnp.concatenate([pool_out, conv_out], axis=-1) @ w_out
    x = x + g1[:, None, :] * mix
    h2 = modulate(rms_norm(x, g_ffn), sh2, sc2)
    hf = h2.reshape(B * L, D)
    idx, wts = route(hf, w_router, b_router)
    routed = routed_experts(hf, idx, wts, w_gate, w_up, w_down)
    shared = (jax.nn.silu(hf @ ws_gate) * (hf @ ws_up)) @ ws_down
    x = x + g2[:, None, :] * (routed + shared).reshape(B, L, D)
    return x, new_pool, new_conv

def setup_inputs(seed: int = 0) -> dict:
    key = jax.random.key(seed)
    ks = jax.random.split(key, 32)
    f32 = jnp.float32
    n = lambda k, shape, s: jax.random.normal(k, shape, f32) * s
    D = D_MODEL
    return {
        "x_prompt": n(ks[0], (BATCH, SEQ, D), 1.0),
        "x_sample": n(ks[1], (DEC_BATCH, DEC_SEQ, D), 1.0),
        "state_pool": n(ks[2], (DEPTH, DEC_BATCH, POOL_BUF, POOL_WIDTH), 1.0),
        "state_conv": n(ks[3], (DEPTH, DEC_BATCH, CONV_BUF, CONV_WIDTH), 1.0),
        "c_prompt": n(ks[4], (BATCH, D), 1.0),
        "c_sample": n(ks[5], (DEC_BATCH, D), 1.0),
        "w_ada": n(ks[6], (DEPTH, D, 6 * D), 0.5 * D ** -0.5),
        "b_ada": n(ks[7], (DEPTH, 6 * D), 0.01),
        "g_mix": 1.0 + n(ks[8], (DEPTH, D), 0.1),
        "w_in": n(ks[9], (DEPTH, D, D_IN), D ** -0.5),
        "w_pool": n(ks[10], (DEPTH, N_POOL_GROUPS, POOL_GROUP, POOL_GROUP), POOL_GROUP ** -0.5),
        "pool_scale": 1.0 + n(ks[11], (DEPTH, POOL_WIDTH), 0.1),
        "w_dw": n(ks[12], (DEPTH, CONV_K, CONV_WIDTH), CONV_K ** -0.5),
        "b_dw": n(ks[13], (DEPTH, CONV_WIDTH), 0.01),
        "ln_g": 1.0 + n(ks[14], (DEPTH, CONV_WIDTH), 0.1),
        "ln_b": n(ks[15], (DEPTH, CONV_WIDTH), 0.01),
        "w_out": n(ks[16], (DEPTH, D_MIX, D), D_MIX ** -0.5),
        "g_ffn": 1.0 + n(ks[17], (DEPTH, D), 0.1),
        "w_router": n(ks[18], (DEPTH, D, N_EXPERTS), D ** -0.5),
        "b_router": n(ks[19], (DEPTH, N_EXPERTS), 0.01),
        "w_gate": n(ks[20], (DEPTH, N_EXPERTS, D, D_EXPERT), D ** -0.5),
        "w_up": n(ks[21], (DEPTH, N_EXPERTS, D, D_EXPERT), D ** -0.5),
        "w_down": n(ks[22], (DEPTH, N_EXPERTS, D_EXPERT, D), D_EXPERT ** -0.5),
        "ws_gate": n(ks[23], (DEPTH, D, D_EXPERT), D ** -0.5),
        "ws_up": n(ks[24], (DEPTH, D, D_EXPERT), D ** -0.5),
        "ws_down": n(ks[25], (DEPTH, D_EXPERT, D), D_EXPERT ** -0.5),
        "w_ada_final": n(ks[26], (D, 2 * D), 0.5 * D ** -0.5),
        "b_ada_final": n(ks[27], (2 * D,), 0.01),
        "g_final": 1.0 + n(ks[28], (D,), 0.1),
    }

def reference(x_prompt, x_sample, state_pool, state_conv, c_prompt, c_sample, w_ada, b_ada, g_mix,
              w_in, w_pool, pool_scale, w_dw, b_dw, ln_g, ln_b, w_out, g_ffn, w_router, b_router,
              w_gate, w_up, w_down, ws_gate, ws_up, ws_down, w_ada_final, b_ada_final, g_final):
    xp, xs = x_prompt, x_sample
    Bp = xp.shape[0]
    sample_valid = min(PAST_LEN, POOL_BUF)
    pool_p, conv_p, pool_s, conv_s = [], [], [], []
    for l in range(DEPTH):
        lw = (w_ada[l], b_ada[l], g_mix[l], w_in[l], w_pool[l], pool_scale[l], w_dw[l], b_dw[l],
              ln_g[l], ln_b[l], w_out[l], g_ffn[l], w_router[l], b_router[l], w_gate[l], w_up[l],
              w_down[l], ws_gate[l], ws_up[l], ws_down[l])
        zp = jnp.zeros((Bp, POOL_BUF, POOL_WIDTH), xp.dtype)
        zc = jnp.zeros((Bp, CONV_BUF, CONV_WIDTH), xp.dtype)
        xp, npp, ncp = layer(xp, c_prompt, zp, zc, 0, *lw)
        xs, nps, ncs = layer(xs, c_sample, state_pool[l], state_conv[l], sample_valid, *lw)
        pool_p.append(npp); conv_p.append(ncp); pool_s.append(nps); conv_s.append(ncs)

    def final(x, c):
        shf, scf = jnp.split(jax.nn.silu(c) @ w_ada_final + b_ada_final, 2, axis=-1)
        return modulate(rms_norm(x, g_final), shf, scf)

    y_prompt = final(xp, c_prompt)
    y_sample = final(xs, c_sample)
    return (y_prompt, y_sample, jnp.stack(pool_p), jnp.stack(conv_p), jnp.stack(pool_s), jnp.stack(conv_s))


_drawn_inputs = setup_inputs


def setup_inputs(seed=0):
    import zlib

    import numpy as np

    out = dict(_drawn_inputs(seed))
    spreads = {}
    factors = {'b_dw': 7.062, 'ln_b': 23.045, 'b_ada_final': 4.337}
    for name, (base, spread) in spreads.items():
        noise = np.random.default_rng([zlib.crc32(name.encode()), seed]).standard_normal(out[name].shape)
        drawn = base * np.exp(spread * noise) if base else spread * noise
        out[name] = __import__('jax').numpy.asarray(drawn.astype(out[name].dtype))
    for name, factor in factors.items():
        out[name] = (out[name] * factor).astype(out[name].dtype)
    return out
```

```python
from contextlib import ExitStack, contextmanager

import concourse.bass as bass
from concourse import mybir

F32 = mybir.dt.float32
BF16 = mybir.dt.bfloat16
I32 = mybir.dt.int32
U32 = mybir.dt.uint32
ACT = mybir.ActivationFunctionType
ALU = mybir.AluOpType
AX = mybir.AxisListType
ds = bass.ds

P = 128
D = 1024
KD = D // P
SEQ = 2048
NS = 8
T = SEQ + NS
TROWS = 18 * P
NC = NS + 1
PW = 512
CH = PW // P
DIN = 3 * PW
ZC = DIN // P
POOLB, CONVB, TAPS = 15, 30, 31
NE, NG, TOPG, TOPK = 64, 8, 4, 8
DE = 256
KE = DE // P
SCALE = 2.5
EPS = 1e-6
BIG = 3.0e38
SUP = 256
TPS = SUP // P
NSUP = SEQ // SUP
NTILE = SEQ // P
EB = -(-T // P)
NCOL = NE * EB + EB + 1
SHCOL = NE * EB
PADCOL = NCOL - 1
MAXB = EB + (T * TOPK) // P + NE
NBT = MAXB + 7
NORD = NE + 1
SBLK = 16
CREP = NE * EB // 16


class Tally:

    def __init__(self):
        self.base, self.n = 0, 0

    @property
    def now(self):
        return self.base + self.n

    def step(self, k=1):
        self.n += k
        return self.now


@contextmanager
def rolled(eng, count, per):
    starts = {t: t.now for t in per}
    with eng.Fori(0, count) as i:
        for t, k in per.items():
            t.base, t.n = starts[t] + i * k, 0
        yield i
        bad = [(t.n, k) for t, k in per.items() if t.n != k]
        assert not bad, bad
    for t, k in per.items():
        t.base, t.n = starts[t] + count * k, 0


class Goal:

    def __init__(self, eng, name, start, step):
        self.eng, self.by, self.reg = eng, step, eng.alloc_register(name)
        eng.reg_mov(self.reg, start)

    def wait(self, sem):
        self.eng.wait_ge(sem, self.reg)
        self.eng.reg_add(self.reg, self.reg, self.by)


def wait(eng, sem, value):
    if isinstance(value, int) and value <= 0:
        return
    eng.wait_ge(sem, value)


def program(nc, a, const, out, stop=9):
    ctx = ExitStack()

    def sem(name):
        return ctx.enter_context(nc.semaphore(name))

    def sb(name, shape, dt=F32, stack=ctx):
        return stack.enter_context(nc.sbuf_tensor("b_" + name, shape, dt))

    def dram(name, shape, dt=F32):
        return nc.dram_tensor(name, shape, dt, kind="Internal").ap()

    def bank(name):
        return ctx.enter_context(nc.psum_tensor(name, [P, 512], F32))

    mod_d = dram("mod_d", (NC, 8 * D))
    x1_d = dram("x1_d", (T, D))
    hf_d = dram("hf_d", (T + P, D))
    acc_d = dram("acc_d", (TROWS, D))
    list_d = dram("list_d", (P * NCOL, 2), I32)
    x_p = a["x_prompt"].rearrange("b t d -> (b t) d")
    x_s = a["x_sample"].rearrange("b t d -> (b t) d")

    tp = [bank("tp0"), bank("tp1")]
    zb = [bank("zb0"), bank("zb1")]
    ly = bank("ly")
    mx = [bank("mx0"), bank("mx1")]
    ms = bank("ms")

    ident = sb("ident", [P, P]); ones = sb("ones", [P, P]); half = sb("half", [P, 1])
    btab = sb("btab", [1, 3, NBT], I32)
    ctab = sb("ctab", [1, NORD], I32)

    names = """const_in c_in small_in win_in wout_in state_in bc_in zero_st init_st edge_st xres_in x1_st h2_st smod_in
        dve_link pool_link csig prep_pe prep_act c_ready mod_filled mod_drained mod1_t aff_ready bc_ready
        xt_filled h_filled tp_drained zp_filled zw_filled zl_filled z_drained ly_filled ly_drained
        mix_filled mix_drained lg_filled lg_drained rk_filled rk_drained xsq xms xrs xn_ready lnv lnr
        x1_ready x1_sq x1_ms x1_rs h2_ready a_ready a_taken d_ready conv_link m_ready pairs_ready
        pool_const dve_const sm_x sm_h sm_state sm_y edge_tp edge_ready
        cnt_filled cnt_ready table_in tables_ready w_landed scatb gu_filled sg_ready hh_ready ht_filled ht_drained
        gx_filled gx_act gx_dve o_filled o_act o_dve f_sum f_sq f_ms f_rs f_aff f_y""".split()
    S = {n: sem(n) for n in names}
    for n in ("ada_in", "adab_in", "xin_in", "scat", "gath", "fin_in", "fin_st"):
        S[n] = [sem(f"{n}0"), sem(f"{n}1")]
    S["modrow_st"] = [sem(f"modrow_st{i}") for i in range(4)]

    front = ExitStack()

    def f(name, shape, dt=F32):
        return sb(name, shape, dt, front)

    tri = f("tri", [P, P])
    poolfix = f("poolfix", [P, CH, 16]); iota64 = f("iota64", [P, NE]); base17 = f("base17", [P, NE])
    thr = f("thr", [NE, EB]); uinc = f("uinc", [NE, NE])
    vecs = f("vecs", [24, P]); vecT = f("vecT", [P, 24]); dwr = f("dwr", [TAPS, PW]); wdw = f("wdw", [P, CH, TAPS])
    router_b = f("router_b", [P, NE]); w_router = f("w_router", [P, KD, NE]); w_pool = f("w_pool", [P, CH, P])
    A1T = f("A1T", [P, KD, NC]); B1T = f("B1T", [P, KD, NC])
    g1b = f("g1b", [P, D]); A2b = f("A2b", [P, D]); B2b = f("B2b", [P, D])
    win = f("win", [P, KD, DIN])
    big = f("big", [P, 2, KD, 512])
    hT = f("hT", [P, KD, SUP])
    av = f("av", [P, CH, SUP]); a_buf = f("a_buf", [P, CH, CONVB + SUP]); u_buf = f("u_buf", [P, CH, POOLB + SUP])
    y = f("y", [P, CH, SUP]); dd = f("dd", [P, CH, SUP]); mixP = f("mixP", [P, CH, SUP]); mixC = f("mixC", [P, TPS, CH, P])
    sgt = f("sgt", [P, 2, SUP]); vv = f("vv", [P, 2, SUP]); pa = f("pa", [P, 2, POOLB + SUP])
    xin = [f("xin0", [P, D]), f("xin1", [P, D])]; xres = f("xres", [P, D]); x1b = f("x1b", [P, D]); h2 = f("h2", [P, D])
    h2T = f("h2T", [P, KD, P]); yn = f("yn", [P, PW]); junk = f("junk", [P, D], BF16)
    st = f("st", [P, 16]); bn6 = f("bn6", [P, 6]); bn2 = f("bn2", [P, 2])
    sg_r = [f("sg_r0", [P, NE]), f("sg_r1", [P, NE])]; sel = f("sel", [P, NE]); m8 = f("m8", [P, NG, 8])
    gsc = f("gsc", [P, 8]); gm = f("gm", [P, 8]); gi = f("gi", [P, 8], U32); gif = f("gif", [P, 8])
    oh4 = f("oh4", [P, NG, TOPG]); gmask = f("gmask", [P, NG]); pen = f("pen", [P, NG])
    oh = f("oh", [P, TOPK, NE]); Mt = f("Mt", [P, NE]); Macc = f("Macc", [P, NE]); prod = f("prod", [P, TOPK, NE])
    wk = f("wk", [P, TOPK]); ri = f("ri", [P, 3, NE], I32); dst = f("dst", [P, NE]); dk = f("dk", [P, TOPK])
    rows = [f("rows0", [P, TOPK], I32), f("rows1", [P, TOPK], I32)]
    pairs = [f("pairs0", [P, TOPK, 2], I32), f("pairs1", [P, TOPK, 2], I32)]
    tokid = f("tokid", [P, 1], I32)
    usm = f("usm", [P, CH, NS]); asm = f("asm", [P, CH, NS]); gsm = f("gsm", [P, CH, NS])
    ysm = f("ysm", [P, CH, NS]); dsm = f("dsm", [P, CH, NS]); xsT = f("xsT", [P, KD, NS])
    cnt = f("cnt", [NE, 1]); nb = f("nb", [NE, 1]); ccum = f("ccum", [NE, 1]); nbt = f("nbt", [NE, EB])
    early = ExitStack()
    c9 = sb("c9", [NC, D], F32, early); cs9 = sb("cs9", [NC, D], F32, early); cT = sb("cT", [P, KD, NC], F32, early)
    mrow = sb("mrow", [NC, 4, 512], F32, early); mbias = sb("mbias", [NC, 2, 512], F32, early)
    lpad = sb("lpad", [P, CREP, 2], I32, early); lsh = sb("lsh", [P, EB + 1, 2], I32, early)
    early.close()
    late = ExitStack()
    full_c = sb("full_c", [P, CH, NS, TAPS], F32, late); full_p = sb("full_p", [P, CH, NS, POOLB + 1], F32, late)
    strow = [sb(f"strow{i}", [P, PW], F32, late) for i in range(3)]
    edge = sb("edge", [CONVB, 4, PW], F32, late)
    late.close()
    front.close()

    moe = ExitStack()

    def g(name, shape, dt=F32):
        return sb(name, shape, dt, moe)

    brow = g("brow", [1, 2, NBT]); biota = g("biota", [NE, NBT]); amat = g("amat", [NE, NBT]); tabf = g("tabf", [1, 5, NBT])
    lt = g("lt", [P, NCOL, 2], I32)
    ltf = lt[:].rearrange("p c w -> p (c w)").bitcast(F32)
    wgu = g("wgu", [P, 2, KD, 2, DE]); wd = g("wd", [P, 2, KE, D])
    xg = [g("xg0", [P, D]), g("xg1", [P, D])]; xT = g("xT", [P, KD, P])
    sgx = [g("sgx0", [P, DE]), g("sgx1", [P, DE])]; hh = g("hh", [P, DE]); hhT = g("hhT", [P, KE, P])
    ob = [g("ob0", [P, D]), g("ob1", [P, D])]
    gidx = [g("gidx0", [P, 1], I32), g("gidx1", [P, 1], I32)]; sidx = [g("sidx0", [P, 1], I32), g("sidx1", [P, 1], I32)]
    moe.close()
    fin = ExitStack()
    _pad = sb("fin_gap", [P, 24 * D], F32, fin)
    g2b = sb("g2b", [P, D], F32, fin); Afb = sb("Afb", [P, D], F32, fin); Bfb = sb("Bfb", [P, D], F32, fin); gfb = sb("gfb", [P, D], F32, fin)
    fa = [sb(f"fa{i}", [P, D], F32, fin) for i in range(2)]; fx = [sb(f"fx{i}", [P, D], F32, fin) for i in range(2)]
    fy = [sb(f"fy{i}", [P, D], F32, fin) for i in range(2)]; fjunk = sb("fjunk", [P, D], BF16, fin); fst = sb("fst", [P, 8], F32, fin);
    fin.close()

    w_ada = a["w_ada"][0].rearrange("(k p) n -> p k n", p=P)
    w_fin = a["w_ada_final"].rearrange("(k p) n -> p k n", p=P)
    b_fin = a["b_ada_final"].rearrange("(o n) -> o n", o=1)
    ada_cols = [(w_ada, a["b_ada"], n * 512) for n in range(12)] + [(w_fin, b_fin, n * 512) for n in range(4)]
    mod_row = lambda m, r0, r1: mod_d[r0:r1, m * D:(m + 1) * D]
    MOD_G1, MOD_SH2, MOD_SC2, MOD_G2, MOD_SHF, MOD_SCF = 2, 3, 4, 5, 6, 7

    block = ctx.enter_context(nc.Block())

    @block.sync
    def _(sp):
        for t, name in ((ident, "ident"), (tri, "tri"), (ones, "ones"), (poolfix, "poolfix"), (iota64, "iota64"),
                        (base17, "base17"), (thr, "thr"), (uinc, "uinc")):
            sp.dma_start(t[:], const[name]).then_inc(S["const_in"], 16)
        sp.dma_start(c9[0:NS, :], a["c_sample"]).then_inc(S["c_in"], 16)
        sp.dma_start(c9[NS:NC, :], a["c_prompt"]).then_inc(S["c_in"], 16)
        for i, name in enumerate(("b_dw", "ln_g", "ln_b", "pool_scale")):
            sp.dma_start(vecs[4 * i:4 * i + 4, :], a[name].rearrange("o (r p) -> (o r) p", p=P)).then_inc(S["small_in"], 16)
        sp.dma_start(vecs[16:24, :], a["g_mix"].rearrange("o (r p) -> (o r) p", p=P)).then_inc(S["small_in"], 16)
        sp.dma_start(dwr[:], a["w_dw"][0]).then_inc(S["small_in"], 16)
        sp.dma_start(router_b[:], a["b_router"].to_broadcast([P, NE])).then_inc(S["small_in"], 16)
        sp.dma_start(w_router[:], a["w_router"][0].rearrange("(k p) n -> p k n", p=P)).then_inc(S["small_in"], 16)
        sp.dma_start(w_pool[:], a["w_pool"][0].rearrange("g c d -> c g d")).then_inc(S["small_in"], 16)

        def load_x(s, j):
            sp.dma_start(xin[j][:], x_p[ds(s * SUP + j * P, P), :]).then_inc(S["xin_in"][j], 16)

        for n in range(SBLK):
            w, b, c0 = ada_cols[n]
            if n >= 2:
                sp.wait_ge(S["mod_filled"], n - 1)
            sp.dma_start(big[:, n % 2, :, :], w[:, :, c0:c0 + 512]).then_inc(S["ada_in"][n % 2], 16)
            if n >= 2:
                sp.wait_ge(S["mod_drained"], n - 1)
            sp.dma_start(mbias[:, n % 2, :], b[0:1, c0:c0 + 512].to_broadcast([NC, 512])).then_inc(S["adab_in"][n % 2], 16)
            if n >= 2:
                sp.dma_start(mod_d[:, (n - 2) * 512:(n - 1) * 512], mrow[:, (n - 2) % 4, :]).then_inc(S["modrow_st"][(n - 2) % 4], 16)
            if n == 1:
                load_x(0, 0)
                load_x(0, 1)
            if n == 3:
                sp.dma_start(win[:], a["w_in"][0].rearrange("(k p) n -> p k n", p=P)).then_inc(S["win_in"], 16)
            if n == 5:
                sp.wait_ge(S["pool_const"], 6)
                sp.dma_start(acc_d.rearrange("(t p) n -> p t n", p=P),
                             x1b[:, :].unsqueeze(1).to_broadcast([P, TROWS // P, D])).then_inc(S["zero_st"], 16)
                sp.dma_start(hf_d[T:T + P, :], x1b[:]).then_inc(S["zero_st"], 16)
                lists = list_d.rearrange("(p c) w -> p (c w)", p=P)
                sp.dma_start(lists[:, 0:2 * SHCOL].rearrange("p (r c) -> p r c", r=16),
                             lpad[:].rearrange("p c w -> p (c w)").unsqueeze(1).to_broadcast([P, 16, 2 * CREP])).then_inc(S["init_st"], 16)
                sp.dma_start(lists[:, 2 * SHCOL:2 * NCOL], lsh[:].rearrange("p c w -> p (c w)")).then_inc(S["init_st"], 16)
        for n in (SBLK - 2, SBLK - 1):
            sp.wait_ge(S["mod_drained"], n + 1)
            sp.dma_start(mod_d[:, n * 512:(n + 1) * 512], mrow[:, n % 4, :]).then_inc(S["modrow_st"][n % 4], 16)
        sp.wait_ge(S["mod_filled"], SBLK)
        for n in range(2):
            sp.dma_start(big[:, n, :, :], a["w_out"][0].rearrange("(k p) n -> p k n", p=P)[:, :, n * 512:(n + 1) * 512]).then_inc(S["wout_in"], 16)
        for q in S["modrow_st"]:
            sp.wait_ge(q, 4 * SBLK)
        sp.dma_start(g1b[:], mod_row(MOD_G1, NS, NC).to_broadcast([P, D])).then_inc(S["bc_in"], 16)
        sp.dma_start(B2b[:], mod_row(MOD_SH2, NS, NC).to_broadcast([P, D])).then_inc(S["bc_in"], 16)
        sp.dma_start(A2b[:], mod_row(MOD_SC2, NS, NC).to_broadcast([P, D])).then_inc(S["bc_in"], 16)
        sp.dma_start(h2[:], a["g_ffn"].to_broadcast([P, D])).then_inc(S["bc_in"], 16)
        sp.wait_ge(S["zero_st"], 32)

        tile = Tally()

        def tile_io(src, nt):
            i = tile.now
            wait(sp, S["x1_ready"], i)
            sp.dma_start(xres[0:nt, :], src).then_inc(S["xres_in"], 16)
            sp.wait_ge(S["x1_ready"], i + 1)
            sp.dma_start(x1_d[ds(i * P, nt), :], x1b[0:nt, :]).then_inc(S["x1_st"], 16)
            sp.wait_ge(S["h2_ready"], i + 1)
            sp.dma_start(hf_d[ds(i * P, nt), :], h2[0:nt, :]).then_inc(S["h2_st"], 16)
            tile.step()

        def step(s, has_next, has_post):
            if has_next:
                for j in range(TPS):
                    sp.wait_ge(S["xt_filled"], 2 * TPS * s + 2 * j + 2)
                    load_x(s + 1, j)
            if has_post:
                for j in range(TPS):
                    tile_io(x_p[ds(tile.now * P, P), :], P)

        step(0, True, False)
        step(1, True, True)
        with rolled(sp, NSUP - 3, {tile: TPS}) as i:
            step(i + 2, True, True)
        step(NSUP - 1, False, True)
        step(NSUP, False, True)
        sp.wait_ge(S["xt_filled"], 2 * NTILE)
        sp.dma_start(xin[0][0:NS, :], x_s).then_inc(S["xin_in"][0], 16)
        sp.dma_start(xin[1][0:NS, :], a["g_ffn"].to_broadcast([NS, D])).then_inc(S["xin_in"][1], 16)
        sp.dma_start(strow[0][0:NS * POOLB, :], a["state_pool"][0].rearrange("b t c -> (b t) c")).then_inc(S["state_in"], 16)
        conv_rows = a["state_conv"][0].rearrange("b t c -> (b t) c")
        for h in range(2):
            sp.dma_start(strow[1 + h][0:4 * CONVB, :], conv_rows[h * 4 * CONVB:(h + 1) * 4 * CONVB, :]).then_inc(S["state_in"], 16)
        sp.dma_start(out[4][0, :, 0:POOLB - 1, :], a["state_pool"][0, :, 1:POOLB, :]).then_inc(S["edge_st"], 16)
        sp.dma_start(out[5][0, :, 0:CONVB - 1, :], a["state_conv"][0, :, 1:CONVB, :]).then_inc(S["edge_st"], 16)
        sp.wait_ge(S["h2_ready"], NTILE)
        for m, t in ((MOD_G1, g1b), (MOD_SH2, B2b), (MOD_SC2, A2b)):
            sp.dma_start(t[0:NS, :], mod_row(m, 0, NS)).then_inc(S["smod_in"], 16)
        tile_io(x_s, NS)
        sp.wait_ge(S["edge_ready"], 4)
        sp.dma_start(out[2][0, 0], edge[0:POOLB, 0, :]).then_inc(S["edge_st"], 16)
        sp.dma_start(out[3][0, 0], edge[0:CONVB, 1, :]).then_inc(S["edge_st"], 16)
        sp.dma_start(out[4][0, :, POOLB - 1, :], edge[0:NS, 2, :]).then_inc(S["edge_st"], 16)
        sp.dma_start(out[5][0, :, CONVB - 1, :], edge[0:NS, 3, :]).then_inc(S["edge_st"], 16)
        sp.wait_ge(S["edge_st"], 96)
        sp.wait_ge(S["x1_st"], 16 * (NTILE + 1))
        sp.wait_ge(S["h2_st"], 16 * (NTILE + 1))
        sp.wait_ge(S["scat"][0], 16 * TOPK * (NSUP + 1))
        sp.wait_ge(S["scat"][1], 16 * TOPK * NSUP)
        sp.wait_ge(S["cnt_ready"], 1)
        sp.wait_ge(S["cnt_filled"], 2)
        sp.dma_start(lt[:].rearrange("p c w -> p (c w)"), list_d.rearrange("(p c) w -> p (c w)", p=P)).then_inc(S["table_in"], 16)
        sp.dma_start(brow[:], const["brow"]).then_inc(S["table_in"], 16)
        sp.dma_start(biota[:], const["biota"]).then_inc(S["table_in"], 16)
        if stop < 2:
            sp.wait_ge(S["table_in"], 48)
            return

        sh = [a["ws_gate"][0], a["ws_up"][0], a["ws_down"][0]]

        def load_w(slot, gate, up, down):
            sp.dma_start(wgu[:, slot, :, 0, :], gate.rearrange("(k p) n -> p k n", p=P)).then_inc(S["w_landed"], 16)
            sp.dma_start(wgu[:, slot, :, 1, :], up.rearrange("(k p) n -> p k n", p=P)).then_inc(S["w_landed"], 16)
            sp.dma_start(wd[:, slot, :, :], down.rearrange("(k p) n -> p k n", p=P)).then_inc(S["w_landed"], 16)

        def expert(e):
            return [a[n][0].rearrange("e d n -> (e d) n")[ds(e * r, r), :] for n, r in (("w_gate", D), ("w_up", D), ("w_down", DE))]

        sp.wait_ge(S["cnt_ready"], 2)
        load_w(0, *sh)
        sp.wait_ge(S["w_landed"], 48)
        load_w(1, *expert(0))
        sp.wait_ge(S["tables_ready"], 1)

        def next_w(e, slot):
            sp.wait_ge(S["w_landed"], 48 * e + 48)
            done = sp.value_load(ctab[0:1, ds(e - 1, 1)], min_val=EB, max_val=MAXB)
            sp.wait_ge(S["o_filled"], done)
            load_w(slot, *expert(e))

        next_w(1, 0)
        with sp.Fori(0, (NE - 2) // 2) as q:
            next_w(2 * q + 2, 1)
            next_w(2 * q + 3, 0)
        sp.wait_ge(S["w_landed"], 48 * NORD)

        turns = (sp.value_load(ctab[0:1, NE:NE + 1], min_val=EB, max_val=MAXB) + 1) // 2
        sp.wait_ge(S["scatb"], turns * 32)
        for m, t in ((MOD_G2, g2b), (MOD_SHF, Bfb), (MOD_SCF, Afb)):
            sp.dma_start(t[:], mod_row(m, NS, NC).to_broadcast([P, D])).then_inc(S["smod_in"], 16)
        sp.dma_start(gfb[:], a["g_final"].rearrange("(o n) -> o n", o=1).to_broadcast([P, D])).then_inc(S["smod_in"], 16)

        def load_f(i, j, nt=P):
            sp.dma_start(fa[j][0:nt, :], acc_d[ds(i * P, nt), :]).then_inc(S["fin_in"][j], 16)
            sp.dma_start(fx[j][0:nt, :], x1_d[ds(i * P, nt), :]).then_inc(S["fin_in"][j], 16)

        load_f(0, 0)
        load_f(1, 1)
        y_p = out[0].rearrange("b t d -> (b t) d")
        with sp.Fori(0, NTILE // 2 - 1) as q:
            for j in range(2):
                sp.wait_ge(S["f_y"], 2 * q + j + 1)
                sp.dma_start(y_p[ds((2 * q + j) * P, P), :], fy[j][:]).then_inc(S["fin_st"][j], 16)
                load_f(2 * q + j + 2, j)
        for j in range(2):
            i = NTILE - 2 + j
            sp.wait_ge(S["f_y"], i + 1)
            sp.dma_start(y_p[ds(i * P, P), :], fy[j][:]).then_inc(S["fin_st"][j], 16)
        load_f(NTILE, 0, NS)
        for m, t in ((MOD_G2, g2b), (MOD_SHF, Bfb), (MOD_SCF, Afb)):
            sp.dma_start(t[0:NS, :], mod_row(m, 0, NS)).then_inc(S["smod_in"], 16)
        sp.wait_ge(S["f_y"], NTILE + 1)
        sp.dma_start(out[1].rearrange("b t d -> (b t) d"), fy[0][0:NS, :]).then_inc(S["fin_st"][0], 16)
        sp.wait_ge(S["fin_st"][0], 16 * (NTILE // 2 + 1))
        sp.wait_ge(S["fin_st"][1], 16 * (NTILE // 2))

    @block.gpsimd
    def _(pool):

        linked = Goal(pool, "pool_linked", 1, 1)
        routed = Goal(pool, "pool_routed", 1, 1)
        added = Goal(pool, "pool_added", 32, 16)

        def chain(ins):
            ins.then_inc(S["pool_link"], 1)
            linked.wait(S["pool_link"])

        G = nc.gpsimd
        G.iota(lpad[:, :, 0], [[0, CREP]], base=T, channel_multiplier=1).then_inc(S["pool_const"], 1)
        G.memset(lpad[:, :, 1], 0).then_inc(S["pool_const"], 1)
        G.iota(lsh[:, :, 0], [[P, EB + 1]], base=0, channel_multiplier=1).then_inc(S["pool_const"], 1)
        pool.wait_ge(S["pool_const"], 3)
        G.iota(lsh[:, EB:EB + 1, 0], [[0, 1]], base=T, channel_multiplier=1).then_inc(S["pool_const"], 1)
        G.memset(lsh[:, :, 1].bitcast(F32), 1.0).then_inc(S["pool_const"], 1)
        G.memset(x1b[:], 0.0).then_inc(S["pool_const"], 1)
        G.memset(half[:], -0.5).then_inc(S["pool_const"], 1)
        G.memset(u_buf[:, :, 0:POOLB], 0.0).then_inc(S["pool_const"], 1)
        G.iota(tokid[:], [[0, 1]], base=-P, channel_multiplier=1).then_inc(S["pool_const"], 1)
        pool.wait_ge(S["pool_const"], 9)

        z, xt, lt_i = Tally(), Tally(), Tally()

        def power(src, dst_, ready, value, done, nt=P):
            pool.wait_ge(ready, value)
            G.tensor_tensor(dst_[0:nt], src[0:nt], half[0:nt, :], ALU.pow).then_inc(done, 1)

        def diff(s, g_, first, post):
            w = 2 << g_
            zu = z.now + (CH if post else 0) + g_
            pool.wait_ge(S["z_drained"], zu + 1)
            cur, n = u_buf[:, g_, :], POOLB + SUP
            for lev in range(g_ + 1):
                sh_ = 1 << lev
                o = pa[:, lev % 2, 0:n - sh_]
                chain(G.tensor_tensor(o, cur[:, sh_:n], cur[:, 0:n - sh_], ALU.add))
                cur, n = pa[:, lev % 2, :], n - sh_
            mean = pa[:, (g_ + 1) % 2, 0:SUP]
            chain(G.tensor_scalar(mean, cur[:, 16 - w:16 - w + SUP], 1.0 / w, None, ALU.mult))
            if first:
                chain(G.tensor_tensor(mean[:, 0:16], mean[:, 0:16], poolfix[:, g_, :], ALU.mult))
            if post:
                pool.wait_ge(S["zp_filled"], CH * (s - 1) + g_ + 1)
            chain(G.tensor_tensor(dd[:, g_, :], mean, u_buf[:, g_, POOLB:POOLB + SUP], ALU.subtract))
            G.tensor_copy(u_buf[:, g_, 0:POOLB], u_buf[:, g_, SUP:SUP + POOLB]).then_inc(S["d_ready"], 1)

        def amul(s, j, post):
            zv = z.now + (CH if post else 0) + CH + 2 * j + 1
            pool.wait_ge(S["z_drained"], zv + 1)
            if post:
                pool.wait_ge(S["a_taken"], s)
            G.tensor_tensor(av[:, j, :], sgt[:, j % 2, :], vv[:, j % 2, :], ALU.mult).then_inc(S["a_ready"], 1)

        def scatter(tile, j, nt=P):
            if isinstance(tile, int):
                pool.wait_ge(S["pairs_ready"], tile + 1)
            else:
                routed.wait(S["pairs_ready"])
            for k in range(TOPK):
                G.indirect_dma_start(list_d, bass.IndirectOffsetOnAxis(ap=rows[j][0:nt, k:k + 1], axis=0),
                                     pairs[j][0:nt, k, :], None).then_inc(S["scat"][j], 16)

        def step(s, has_in, has_next, has_post, first=False):
            if has_in:
                diff(s, 0, first, has_post); diff(s, 1, first, has_post)
                amul(s, 0, has_post)
                diff(s, 2, first, has_post)
                amul(s, 1, has_post)
                diff(s, 3, first, has_post)
                amul(s, 2, has_post); amul(s, 3, has_post)
            z.step((CH if has_post else 0) + (ZC if has_in else 0) + (TPS if has_post else 0))
            if has_next:
                for j in range(TPS):
                    power(st[:, 2 + j:3 + j], st[:, 4 + j:5 + j], S["xms"], xt.step(), S["xrs"])
            if has_post:
                for j in range(TPS):
                    power(st[:, 6:7], st[:, 7:8], S["lnv"], lt_i.now + j + 1, S["lnr"])
                for j in range(TPS):
                    power(st[:, 9:10], st[:, 10:11], S["x1_ms"], lt_i.step(), S["x1_rs"])
                for j in range(TPS):
                    scatter(lt_i.now - TPS + j, j)

        for j in range(TPS):
            power(st[:, 2 + j:3 + j], st[:, 4 + j:5 + j], S["xms"], xt.step(), S["xrs"])
        pool.wait_ge(S["const_in"], 128)
        pool.wait_ge(S["init_st"], 32)
        step(0, True, True, False, True)
        with rolled(pool, NSUP - 2, {z: CH + ZC + TPS, xt: TPS, lt_i: TPS}) as i:
            step(i + 1, True, True, True)
        step(NSUP - 1, True, False, True)
        step(NSUP, False, False, True)
        power(st[:, 2:3], st[:, 4:5], S["xms"], xt.step(), S["xrs"], NS)
        power(st[:, 6:7], st[:, 7:8], S["lnv"], lt_i.now + 1, S["lnr"], NS)
        power(st[:, 9:10], st[:, 10:11], S["x1_ms"], lt_i.step(), S["x1_rs"], NS)
        scatter(NTILE, 0, NS)
        pool.wait_ge(S["scat"][0], 16 * TOPK * (NSUP + 1))
        pool.wait_ge(S["scat"][1], 16 * TOPK * NSUP)
        if stop < 2:
            return

        pool.wait_ge(S["tables_ready"], 1)
        pool.wait_ge(S["table_in"], 48)
        nblk = pool.value_load(ctab[0:1, NE:NE + 1], min_val=EB, max_val=MAXB)

        def ids(b, dst_):
            col = pool.value_load(btab[0:1, 0, ds(b, 1)], min_val=0, max_val=PADCOL)
            G.tensor_copy(dst_[:], lt[:, ds(col, 1), 0]).then_inc(S["pool_link"], 1)
            linked.wait(S["pool_link"])

        def gather(b, j):
            G.indirect_dma_start(xg[j][:], None, hf_d, bass.IndirectOffsetOnAxis(ap=gidx[j][:, 0:1], axis=0)).then_inc(S["gath"][j], 16)

        pool.wait_ge(S["cnt_ready"], 2)
        for b in range(2):
            ids(b, gidx[b])
            gather(b, b)
        pool.wait_ge(S["gx_filled"], 2)
        ids(2, gidx[0])
        gather(2, 0)

        def turn(q):
            for h in range(2):
                b = 2 * q + 1 + h
                j = (1 + h) % 2
                pool.wait_ge(S["gx_filled"], 2 * b + 2)
                ids(b + 2, gidx[j])
                gather(b + 2, j)
                ids(b - 1, sidx[1 - j])
                pool.wait_ge(S["o_act"], b)
                pool.wait_ge(S["o_dve"], b)
                if isinstance(q, int):
                    wait(pool, S["scatb"], 16 * (b - 1))
                else:
                    added.wait(S["scatb"])
                G.indirect_dma_start(acc_d, bass.IndirectOffsetOnAxis(ap=sidx[1 - j][:, 0:1], axis=0),
                                     ob[1 - j][:], None, compute_op=ALU.add).then_inc(S["scatb"], 16)

        turn(0)
        with pool.Fori(0, (MAXB - 1) // 2) as q:
            with pool.If(2 * q + 2 < nblk):
                turn(q + 1)
        pool.wait_ge(S["smod_in"], 16 * 7)

        def turn(q):
            for j in range(2):
                power(fst[:, 2 + j:3 + j], fst[:, 4 + j:5 + j], S["f_ms"], 2 * q + j + 1, S["f_rs"])
                pool.wait_ge(S["f_aff"], 2 * q + j + 1)
                wait(pool, S["fin_st"][j], 16 * q)
                G.tensor_tensor(fy[j][:], fa[j][:], Bfb[:], ALU.add).then_inc(S["f_y"], 1)

        turn(0)
        with pool.Fori(0, NTILE // 2 - 1) as q:
            turn(q + 1)
        power(fst[:, 2:3], fst[:, 4:5], S["f_ms"], NTILE + 1, S["f_rs"], NS)
        pool.wait_ge(S["f_aff"], NTILE + 1)
        pool.wait_ge(S["fin_st"][0], 16 * (NTILE // 2))
        G.tensor_tensor(fy[0][0:NS, :], fa[0][0:NS, :], Bfb[0:NS, :], ALU.add).then_inc(S["f_y"], 1)

    @block.scalar
    def _(act):
        A = nc.scalar
        tpu, z, xt, ti, wn, zp = Tally(), Tally(), Tally(), Tally(), Tally(), Tally()
        act.wait_ge(S["c_in"], 32)
        A.activation(cs9[:], c9[:], ACT.Sigmoid).then_inc(S["csig"], 1)
        act.wait_ge(S["prep_pe"], 1)
        A.copy(cT[:].rearrange("p k c -> p (k c)"), ly[:, 0:KD * NC]).then_inc(S["prep_act"], 1)
        act.wait_ge(S["prep_pe"], 2)
        A.copy(vecT[:], ms[:, 0:24]).then_inc(S["prep_act"], 1)
        A.copy(wdw[:].rearrange("p c t -> p (c t)"), ms[:, 32:32 + CH * TAPS]).then_inc(S["prep_act"], 1)

        nx, n1 = Tally(), Tally()

        def square(src, dst_, done, nt=P):
            wait(act, S["xsq"], nx.now)
            wait(act, S["x1_sq"], n1.now)
            (nx if done is S["xsq"] else n1).step()
            A.activation(junk[0:nt, :], src[0:nt, :], ACT.Square, accum_out=dst_[0:nt]).then_inc(done, 1)

        def x_square(j, count, nt=P):
            act.wait_ge(S["xin_in"][j], 16 * count)
            square(xin[j], st[:, j:j + 1], S["xsq"], nt)

        def xt_drain(j):
            n = xt.now
            for h in range(2):
                act.wait_ge(S["xt_filled"], 2 * n + h + 1)
                for kk in range(4):
                    k = 4 * h + kk
                    last = A.activation(hT[:, k, j * P:(j + 1) * P], tp[h][:, kk * P:(kk + 1) * P], ACT.Identity,
                                        scale=A1T[:, k, NS:NC], bias=B1T[:, k, NS:NC])
                last.then_inc(S["tp_drained"], 1)
            xt.step(); tpu.step()

        def pool_drain(nt=SUP):
            for g_ in range(CH):
                act.wait_ge(S["zp_filled"], zp.step())
                A.activation(mixP[:, g_, 0:nt], zb[z.n % 2][:, 0:nt], ACT.Copy, scale=vecT[:, 12 + g_:13 + g_]).then_inc(S["z_drained"], 1)
                z.step()

        def win_drain(s, first):
            for g_ in range(CH):
                act.wait_ge(S["zw_filled"], wn.step())
                if not first:
                    act.wait_ge(S["d_ready"], CH * (s - 1) + g_ + 1)
                A.copy(u_buf[:, g_, POOLB:POOLB + SUP], zb[z.n % 2][:, 0:SUP]).then_inc(S["z_drained"], 1)
                z.step()
            for j in range(CH):
                act.wait_ge(S["zw_filled"], wn.step())
                if not (first and j < 2):
                    act.wait_ge(S["a_ready"], CH * s + j - 1)
                A.activation(sgt[:, j % 2, :], zb[z.n % 2][:, 0:SUP], ACT.Sigmoid).then_inc(S["z_drained"], 1)
                z.step()
                act.wait_ge(S["zw_filled"], wn.step())
                A.copy(vv[:, j % 2, :], zb[z.n % 2][:, 0:SUP]).then_inc(S["z_drained"], 1)
                z.step()

        def ln_drain(j, nt=P):
            act.wait_ge(S["zl_filled"], ti.now + j + 1)
            for c in range(CH):
                last = A.activation(mixC[:, j, c, 0:nt], zb[z.n % 2][:, c * P:c * P + nt], ACT.Silu,
                                    scale=vecT[:, 4 + c:5 + c], bias=vecT[:, 8 + c:9 + c])
            last.then_inc(S["z_drained"], 1)
            z.step()

        def x1_square(j, nt=P):
            act.wait_ge(S["x1_ready"], ti.now + j + 1)
            square(x1b, st[:, 8:9], S["x1_sq"], nt)

        def h_drain(j, nt=P):
            for h in range(2):
                act.wait_ge(S["h_filled"], 2 * (ti.now + j) + h + 1)
                A.copy(h2T[:, 4 * h:4 * h + 4, 0:nt], tp[h][:].rearrange("p (k t) -> p k t", k=4)[:, :, 0:nt]).then_inc(S["tp_drained"], 1)
            tpu.step()

        def gate_sigmoid(j, first, nt=P):
            act.wait_ge(S["lg_filled"], ti.now + j + 1)
            if not first:
                act.wait_ge(S["pairs_ready"], ti.now + j - 1)
            A.activation(sg_r[j][0:nt, :], ms[0:nt, 0:NE], ACT.Sigmoid).then_inc(S["lg_drained"], 1)

        def step(s, has_in, has_next, has_post, first=False, second=False):
            if has_post:
                pool_drain()
            if has_in:
                win_drain(s, first)
            if has_next:
                for j in range(TPS):
                    x_square(j, s + 2)
                for j in range(TPS):
                    xt_drain(j)
            if has_post:
                for j in range(TPS):
                    ln_drain(j)
                x1_square(0)
                x1_square(1)
                for j in range(TPS):
                    h_drain(j)
                    gate_sigmoid(j, second)
                ti.step(TPS)

        x_square(0, 1)
        x_square(1, 1)
        act.wait_ge(S["aff_ready"], 2)
        for j in range(TPS):
            xt_drain(j)
        step(0, True, True, False, first=True)
        step(1, True, True, True, second=True)
        with rolled(act, NSUP - 3, {tpu: 2 * TPS, z: CH + ZC + TPS, xt: TPS, ti: TPS, wn: ZC, zp: CH, nx: TPS, n1: TPS}) as i:
            step(i + 2, True, True, True)
        step(NSUP - 1, True, False, True)
        step(NSUP, False, False, True)
        x_square(0, NSUP + 1, NS)
        for h in range(2):
            act.wait_ge(S["xt_filled"], 2 * NTILE + h + 1)
            A.copy(xsT[:, 4 * h:4 * h + 4, :], tp[h][:].rearrange("p (k t) -> p k t", k=4)[:, :, 0:NS]).then_inc(S["tp_drained"], 1)
        act.wait_ge(S["zw_filled"], wn.step())
        zv = zb[z.n % 2][:, 0:ZC * NS].rearrange("p (c t) -> p c t", c=ZC)
        A.copy(usm[:], zv[:, 0:CH, :])
        A.copy(asm[:], zv[:, CH:2 * CH, :])
        A.activation(gsm[:], zv[:, 2 * CH:3 * CH, :], ACT.Sigmoid).then_inc(S["z_drained"], 1)
        z.step()
        for i in range(3):
            act.wait_ge(S["edge_tp"], i + 1)
            src = zb[z.n % 2][:].rearrange("p (c r) -> p c r", c=CH)
            if i == 0:
                v_, d_ = src[:, :, 0:NS * POOLB].rearrange("p c (b t) -> p c b t", b=NS), full_p[:, :, :, 0:POOLB]
            else:
                v_, d_ = src[:, :, 0:4 * CONVB].rearrange("p c (b t) -> p c b t", b=4), full_c[:, :, 4 * i - 4:4 * i, 0:CONVB]
            for c in range(CH):
                last = A.copy(d_[:, c], v_[:, c])
            last.then_inc(S["z_drained"], 1)
            z.step()
        for i, n in enumerate((POOLB, CONVB, NS, NS)):
            act.wait_ge(S["edge_tp"], 4 + i)
            A.copy(edge[0:n, i, :], zb[z.n % 2][0:n, :]).then_inc(S["edge_ready"], 1)
            z.step()
        pool_drain(NS)
        ln_drain(0, NS)
        x1_square(0, NS)
        h_drain(0, NS)
        gate_sigmoid(0, False, NS)
        if stop < 2:
            return

        act.wait_ge(S["tables_ready"], 1)
        nblk = act.value_load(ctab[0:1, NE:NE + 1], min_val=EB, max_val=MAXB)

        def silu(b, j):
            act.wait_ge(S["gu_filled"], b + 1)
            A.activation(sgx[j][:], zb[j][:, 0:DE], ACT.Silu).then_inc(S["sg_ready"], 1)

        def gx(b):
            act.wait_ge(S["gx_filled"], 2 * b + 1)
            A.copy(xT[:, 0:4, :], tp[0][:].rearrange("p (k t) -> p k t", k=4)).then_inc(S["gx_act"], 1)

        def ht(b):
            act.wait_ge(S["ht_filled"], b + 1)
            A.copy(hhT[:].rearrange("p k t -> p (k t)"), ly[:, 0:DE]).then_inc(S["ht_drained"], 1)

        gx(0)
        silu(0, 0)
        gx(1)
        ht(0)

        def turn(q):
            for h in range(2):
                b, j = 2 * q + 1 + h, (1 + h) % 2
                silu(b, j)
                gx(b + 1)
                act.wait_ge(S["o_filled"], b)
                wait(act, S["scatb"], 16 * (b - 2))
                A.copy(ob[1 - j][:, 0:512], mx[0][:]).then_inc(S["o_act"], 1)
                ht(b)

        turn(0)
        with act.Fori(0, (MAXB - 1) // 2) as q:
            with act.If(2 * q + 2 < nblk):
                turn(q + 1)

        act.wait_ge(S["smod_in"], 16 * 7)

        def fsq(i, j, nt=P):
            act.wait_ge(S["f_sum"], i + 1)
            A.activation(fjunk[0:nt, :], fa[j][0:nt, :], ACT.Square, accum_out=fst[0:nt, j:j + 1]).then_inc(S["f_sq"], 1)

        with act.Fori(0, NTILE // 2) as q:
            for j in range(2):
                fsq(2 * q + j, j)
        fsq(NTILE, 0, NS)

    @block.vector
    def _(dve):
        V = nc.vector
        cv, xt, ti = Tally(), Tally(), Tally()
        linked = Goal(dve, "dve_linked", 1, 1)

        def chain(ins):
            ins.then_inc(S["dve_link"], 1)
            linked.wait(S["dve_link"])

        V.memset(a_buf[:], 0.0).then_inc(S["dve_const"], 1)
        V.memset(Macc[:], 0.0).then_inc(S["dve_const"], 1)
        dve.wait_ge(S["dve_const"], 2)
        dve.wait_ge(S["csig"], 1)
        dve.wait_ge(S["c_in"], 32)
        V.tensor_tensor(c9[:], c9[:], cs9[:], ALU.mult).then_inc(S["c_ready"], 1)

        def mod_drain(n):
            dve.wait_ge(S["mod_filled"], n + 1)
            dve.wait_ge(S["adab_in"][n % 2], 16 * (n // 2 + 1))
            if n >= 4:
                dve.wait_ge(S["modrow_st"][n % 4], 16 * (n // 4))
                if n < 8:
                    dve.wait_ge(S["mod1_t"], 1)
            V.tensor_tensor(mrow[:, n % 4, :], zb[n % 2][0:NC, :], mbias[:, n % 2, :], ALU.add).then_inc(S["mod_drained"], 1)

        for n in range(4):
            mod_drain(n)
        dve.wait_ge(S["mod1_t"], 1)
        dve.wait_ge(S["prep_act"], 2)
        V.tensor_copy(B1T[:].rearrange("p k c -> p (k c)"), tp[0][:, 0:KD * NC]).then_inc(S["aff_ready"], 1)
        for k in range(KD):
            last = V.tensor_scalar(A1T[:, k, :], tp[0][:, (KD + k) * NC:(KD + k + 1) * NC], 1.0, vecT[:, 16 + k:17 + k], ALU.add, ALU.mult)
        last.then_inc(S["aff_ready"], 1)

        def xn_ms(j, nt=P):
            dve.wait_ge(S["xsq"], xt.now + 1)
            V.tensor_scalar(st[0:nt, 2 + j:3 + j], st[0:nt, j:j + 1], 1.0 / D, EPS, ALU.mult, ALU.add).then_inc(S["xms"], 1)
            xt.step()

        def xn(j, n, nt=P):
            dve.wait_ge(S["xrs"], n)
            V.tensor_scalar(xin[j][0:nt, :], xin[j][0:nt, :], st[0:nt, 4 + j:5 + j], None, ALU.mult).then_inc(S["xn_ready"], 1)

        def conv(p, first):
            dve.wait_ge(S["a_ready"], CH * p + CH)
            if not first:
                chain(V.tensor_copy(a_buf[:, :, 0:CONVB], a_buf[:, :, SUP:SUP + CONVB]))
            V.tensor_copy(a_buf[:, :, CONVB:CONVB + SUP], av[:]).then_inc(S["a_taken"], 1)
            dve.wait_ge(S["a_taken"], p + 1)
            if not first:
                dve.wait_ge(S["ly_filled"], ti.now)
            for k in range(TAPS):
                for c in range(CH):
                    win_ = a_buf[:, c, k:k + SUP]
                    if k == 0:
                        ins = V.tensor_scalar(y[:, c, :], win_, wdw[:, c, 0:1], vecT[:, c:c + 1], ALU.mult, ALU.add)
                    else:
                        dve.wait_ge(S["conv_link"], cv.now - CH + 1)
                        ins = V.scalar_tensor_tensor(y[:, c, :], win_, wdw[:, c, k:k + 1], y[:, c, :], ALU.mult, ALU.add)
                    ins.then_inc(S["conv_link"], 1)
                    cv.step()

        def norm(i, nt=P):
            dve.wait_ge(S["ly_filled"], i + 1)
            chain(V.bn_stats(bn6[0:nt, :], ly[0:nt, :]))
            chain(V.bn_aggr(bn2[0:nt, :], bn6[0:nt, :]))
            V.tensor_scalar(st[0:nt, 6:7], bn2[0:nt, 1:2], EPS, None, ALU.add).then_inc(S["lnv"], 1)
            dve.wait_ge(S["lnr"], i + 1)
            V.tensor_scalar(yn[0:nt, :], ly[0:nt, :], bn2[0:nt, 0:1], st[0:nt, 7:8], ALU.subtract, ALU.mult).then_inc(S["ly_drained"], 1)

        def residual(i, first, nt=P):
            dve.wait_ge(S["mix_filled"], i + 1)
            dve.wait_ge(S["xres_in"], 16 * i + 16)
            if not first:
                dve.wait_ge(S["x1_st"], 16 * i)
            for n in range(2):
                last = V.tensor_tensor(x1b[0:nt, n * 512:(n + 1) * 512], mx[n][0:nt, :], g1b[0:nt, n * 512:(n + 1) * 512], ALU.mult)
            last.then_inc(S["mix_drained"], 1)
            dve.wait_ge(S["mix_drained"], i + 1)
            V.tensor_tensor(x1b[0:nt, :], x1b[0:nt, :], xres[0:nt, :], ALU.add).then_inc(S["x1_ready"], 1)

        def mixer_in(i, first, nt=P):
            dve.wait_ge(S["x1_sq"], i + 1)
            V.tensor_scalar(st[0:nt, 9:10], st[0:nt, 8:9], 1.0 / D, EPS, ALU.mult, ALU.add).then_inc(S["x1_ms"], 1)
            dve.wait_ge(S["x1_rs"], i + 1)
            if not first:
                dve.wait_ge(S["h2_st"], 16 * i)
                dve.wait_ge(S["h_filled"], 2 * i)
            chain(V.scalar_tensor_tensor(h2[0:nt, :], x1b[0:nt, :], st[0:nt, 10:11], A2b[0:nt, :], ALU.mult, ALU.mult))
            V.tensor_tensor(h2[0:nt, :], h2[0:nt, :], B2b[0:nt, :], ALU.add).then_inc(S["h2_ready"], 1)

        def route(i, j, nt=P):
            dve.wait_ge(S["lg_drained"], i + 1)
            s_ = sg_r[j]
            n = slice(0, nt)
            chain(V.tensor_tensor(sel[n, :], s_[n, :], router_b[n, :], ALU.add))
            for q in range(NG):
                last = V.max(m8[n, q, :], sel[n, 8 * q:8 * q + 8])
            chain(last)
            chain(V.tensor_tensor(gsc[n, :], m8[n, :, 0], m8[n, :, 1], ALU.add))
            chain(V.max(gm[n, :], gsc[n, :]))
            chain(V.max_index(gi[n, :], gm[n, :], gsc[n, :]))
            chain(V.tensor_copy(gif[n, :], gi[n, :]))
            chain(V.tensor_tensor(oh4[n], iota64[n, 0:NG].unsqueeze(2).to_broadcast([nt, NG, TOPG]),
                                  gif[n, 0:TOPG].unsqueeze(1).to_broadcast([nt, NG, TOPG]), ALU.is_equal))
            chain(V.tensor_reduce(gmask[n, :], oh4[n], AX.X, ALU.add))
            chain(V.tensor_scalar(pen[n, :], gmask[n, :], 1.0, BIG, ALU.subtract, ALU.mult))
            sel3 = sel[n, :].rearrange("p (g e) -> p g e", g=NG)
            chain(V.tensor_tensor(sel3, sel3, gmask[n, :].unsqueeze(2).to_broadcast([nt, NG, 8]), ALU.mult))
            chain(V.tensor_tensor(sel3, sel3, pen[n, :].unsqueeze(2).to_broadcast([nt, NG, 8]), ALU.add))
            chain(V.max(gm[n, :], sel[n, :]))
            chain(V.max_index(gi[n, :], gm[n, :], sel[n, :]))
            chain(V.tensor_copy(gif[n, :], gi[n, :]))
            chain(V.tensor_tensor(oh[n], iota64[n, :].unsqueeze(1).to_broadcast([nt, TOPK, NE]),
                                  gif[n, :].unsqueeze(2).to_broadcast([nt, TOPK, NE]), ALU.is_equal))
            V.tensor_reduce(Mt[n, :], oh[n].rearrange("p k e -> p e k"), AX.X, ALU.add).then_inc(S["m_ready"], 1)
            chain(V.tensor_tensor(prod[n], oh[n], s_[n, :].unsqueeze(1).to_broadcast([nt, TOPK, NE]), ALU.mult))
            chain(V.tensor_reduce(wk[n, :], prod[n], AX.X, ALU.add))
            chain(V.tensor_reduce(st[n, 11:12], wk[n, :], AX.X, ALU.add))
            chain(V.reciprocal(st[n, 12:13], st[n, 11:12]))
            chain(V.tensor_scalar(tokid[:], tokid[:], float(P), None, ALU.add))
            pj = pairs[j]
            V.tensor_copy(pj[n, :, 0], tokid[n, :].to_broadcast([nt, TOPK]))
            chain(V.tensor_scalar(pj[n, :, 1].bitcast(F32), wk[n, :], st[n, 12:13], SCALE, ALU.mult, ALU.mult))

        def slots(i, j, nt=P):
            n = slice(0, nt)
            dve.wait_ge(S["rk_filled"], i + 1)
            V.tensor_copy(ri[n, 0, :], ms[n, NE:2 * NE]).then_inc(S["rk_drained"], 1)
            chain(V.tensor_tensor(Macc[n, :], Macc[n, :], Mt[n, :], ALU.add))
            dve.wait_ge(S["rk_drained"], i + 1)
            V.tensor_single_scalar(ri[n, 1, :], ri[n, 0, :], P - 1, ALU.bitwise_and)
            chain(V.tensor_single_scalar(ri[n, 2, :], ri[n, 0, :], 7, ALU.arith_shift_right))
            chain(V.tensor_scalar(dst[n, :], ri[n, 1, :], float(NCOL), None, ALU.mult))
            chain(V.tensor_tensor(dst[n, :], dst[n, :], ri[n, 2, :], ALU.add))
            chain(V.tensor_tensor(dst[n, :], dst[n, :], base17[n, :], ALU.add))
            chain(V.tensor_tensor(prod[n], oh[n], dst[n, :].unsqueeze(1).to_broadcast([nt, TOPK, NE]), ALU.mult))
            chain(V.tensor_reduce(dk[n, :], prod[n], AX.X, ALU.add))
            V.tensor_copy(rows[j][n, :], dk[n, :]).then_inc(S["pairs_ready"], 1)

        def step(s, has_next, has_post, first=False, kind=""):
            if has_post:
                conv(s - 1, kind == "second")
            if has_next:
                for j in range(TPS):
                    xn_ms(j)
                for j in range(TPS):
                    xn(j, xt.now - 1 + j)
            if has_post:
                if kind == "second":
                    bcast(h2)
                for j in range(TPS):
                    norm(ti.now + j)
                for j in range(TPS):
                    residual(ti.now + j, kind == "second" and j == 0)
                    mixer_in(ti.now + j, kind == "second" and j == 0)
                for j in range(TPS):
                    if not kind == "second":
                        dve.wait_ge(S["scat"][j], tix[0](s))
                    route(ti.now + j, j)
                    slots(ti.now + j, j)
                ti.step(TPS)

        def bcast(gain, nt=P, sem_=None):
            dve.wait_ge(S["bc_in"], 64)
            chain(V.scalar_tensor_tensor(A2b[0:nt, :], A2b[0:nt, :], 1.0, gain[0:nt, :], ALU.add, ALU.mult))

        tix = [lambda s: 16 * TOPK * (s - 1)]

        for j in range(TPS):
            xn_ms(j)
        for j in range(TPS):
            xn(j, j + 1)
        for n in range(4, SBLK):
            mod_drain(n)
        dve.wait_ge(S["const_in"], 128)
        dve.wait_ge(S["small_in"], 144)
        dve.wait_ge(S["prep_act"], 3)
        dve.wait_ge(S["pool_const"], 9)
        dve.wait_ge(S["zero_st"], 32)
        step(0, True, False)
        step(1, True, True, kind="second")
        with rolled(dve, NSUP - 3, {cv: CH * TAPS, xt: TPS, ti: TPS}) as i:
            step(i + 2, True, True)
        step(NSUP - 1, False, True)
        step(NSUP, False, True)
        xn_ms(0, NS)
        xn(0, NTILE + 1, NS)
        dve.wait_ge(S["tp_drained"], 2 * (2 * NTILE + 1))
        chain(V.tensor_tensor(xsT[:], xsT[:], A1T[:, :, 0:NS], ALU.mult))
        V.tensor_tensor(hT[:, :, 0:NS], xsT[:], B1T[:, :, 0:NS], ALU.add).then_inc(S["sm_h"], 1)
        zs = NSUP * (CH + ZC + TPS)
        dve.wait_ge(S["z_drained"], zs + 1)
        chain(V.tensor_tensor(asm[:], asm[:], gsm[:], ALU.mult))
        dve.wait_ge(S["z_drained"], zs + 4)
        chain(V.tensor_copy(full_c[:, :, :, CONVB], asm[:]))
        chain(V.tensor_copy(full_p[:, :, :, POOLB], usm[:]))
        for c in range(CH):
            w = 2 << c
            pc = prod[:].rearrange("p k e -> p (k e)")[:, 0:NS * TAPS].rearrange("p (b t) -> p b t", b=NS)
            chain(V.tensor_tensor(pc, full_c[:, c], wdw[:, c, :].unsqueeze(1).to_broadcast([P, NS, TAPS]), ALU.mult))
            chain(V.tensor_reduce(ysm[:, c, :], pc, AX.X, ALU.add))
            chain(V.tensor_scalar(ysm[:, c, :], ysm[:, c, :], vecT[:, c:c + 1], None, ALU.add))
            chain(V.tensor_reduce(dsm[:, c, :], full_p[:, c, :, 16 - w:16], AX.X, ALU.add))
            last = V.scalar_tensor_tensor(dsm[:, c, :], dsm[:, c, :], 1.0 / w, usm[:, c, :], ALU.mult, ALU.subtract)
            if c < CH - 1:
                chain(last)
        last.then_inc(S["sm_y"], 1)
        dve.wait_ge(S["smod_in"], 48)
        dve.wait_ge(S["xin_in"][1], 16 * (NSUP + 1))
        chain(V.scalar_tensor_tensor(A2b[0:NS, :], A2b[0:NS, :], 1.0, xin[1][0:NS, :], ALU.add, ALU.mult))
        norm(NTILE, NS)
        residual(NTILE, False, NS)
        mixer_in(NTILE, False, NS)
        dve.wait_ge(S["scat"][0], 16 * TOPK * NSUP)
        route(NTILE, 0, NS)
        slots(NTILE, 0, NS)
        dve.wait_ge(S["cnt_filled"], 1)
        chain(V.tensor_copy(cnt[:], ms[0:NE, 0:1]))
        chain(V.tensor_scalar(nbt[:], thr[:], cnt[:, 0:1], None, ALU.is_lt))
        V.tensor_reduce(nb[:], nbt[:], AX.X, ALU.add).then_inc(S["cnt_ready"], 1)
        dve.wait_ge(S["cnt_filled"], 2)
        chain(V.tensor_scalar(ccum[:], ms[0:NE, 0:1], float(EB), None, ALU.add))
        V.memset(ctab[0:1, 0:1], EB)
        chain(V.tensor_scalar(ctab[0:1, 1:NORD], ms[0:1, NE:2 * NE], float(EB), None, ALU.add))
        dve.wait_ge(S["table_in"], 48)
        V.tensor_scalar(amat[:], biota[:], ccum[:, 0:1], None, ALU.is_ge).then_inc(S["cnt_ready"], 1)
        dve.wait_ge(S["cnt_filled"], 3)
        e_, s_, cb, mk = tabf[0:1, 0, :], tabf[0:1, 1, :], brow[0:1, 0, :], brow[0:1, 1, :]
        t2, t3, t4 = tabf[0:1, 2, :], tabf[0:1, 3, :], tabf[0:1, 4, :]
        V.tensor_copy(e_, ms[0:1, 0:NBT])
        chain(V.tensor_copy(s_, zb[0][0:1, 0:NBT]))
        chain(V.tensor_scalar(t2, e_, float(EB), None, ALU.mult))
        chain(V.tensor_tensor(t2, t2, cb, ALU.add))
        chain(V.tensor_tensor(t2, t2, s_, ALU.subtract))
        chain(V.tensor_scalar(t3, e_, float(NE), None, ALU.is_ge))
        chain(V.tensor_scalar(t4, t2, -1.0, float(PADCOL), ALU.mult, ALU.add))
        chain(V.tensor_tensor(t4, t4, t3, ALU.mult))
        chain(V.tensor_tensor(t2, t2, t4, ALU.add))
        V.tensor_copy(btab[0:1, 0, :], t2)
        chain(V.tensor_scalar(t3, e_, 1.0, float(NE), ALU.add, ALU.min))
        chain(V.tensor_tensor(t3, t3, mk, ALU.mult))
        chain(V.tensor_copy(btab[0:1, 1, :], t3))
        V.tensor_single_scalar(btab[0:1, 2, :], btab[0:1, 1, :], 1, ALU.bitwise_and).then_inc(S["tables_ready"], 1)
        dve.wait_ge(S["tables_ready"], 1)
        if stop < 2:
            return

        nblk = dve.value_load(ctab[0:1, NE:NE + 1], min_val=EB, max_val=MAXB)

        def hidden(b, j):
            col = dve.value_load(btab[0:1, 0, ds(b, 1)], min_val=0, max_val=PADCOL)
            dve.wait_ge(S["sg_ready"], b + 1)
            V.scalar_tensor_tensor(hh[:], sgx[j][:], ltf[:, ds(2 * col + 1, 1)], zb[j][:, DE:2 * DE], ALU.mult, ALU.mult).then_inc(S["hh_ready"], 1)

        def gx(b):
            dve.wait_ge(S["gx_filled"], 2 * b + 2)
            V.tensor_copy(xT[:, 4:8, :], tp[1][:].rearrange("p (k t) -> p k t", k=4)).then_inc(S["gx_dve"], 1)

        gx(0)
        hidden(0, 0)
        gx(1)

        def turn(q):
            for h in range(2):
                b, j = 2 * q + 1 + h, (1 + h) % 2
                dve.wait_ge(S["ht_filled"], b)
                hidden(b, j)
                gx(b + 1)
                dve.wait_ge(S["o_filled"], b)
                wait(dve, S["scatb"], 16 * (b - 2))
                V.tensor_copy(ob[1 - j][:, 512:1024], mx[1][:]).then_inc(S["o_dve"], 1)

        turn(0)
        with dve.Fori(0, (MAXB - 1) // 2) as q:
            with dve.If(2 * q + 2 < nblk):
                turn(q + 1)

        dve.wait_ge(S["smod_in"], 16 * 7)
        chain(V.scalar_tensor_tensor(Afb[:], Afb[:], 1.0, gfb[:], ALU.add, ALU.mult))

        def final(i, j, nt=P):
            dve.wait_ge(S["fin_in"][j], f_loads(i, j))
            chain(V.tensor_tensor(fa[j][0:nt, :], fa[j][0:nt, :], g2b[0:nt, :], ALU.mult))
            V.tensor_tensor(fa[j][0:nt, :], fa[j][0:nt, :], fx[j][0:nt, :], ALU.add).then_inc(S["f_sum"], 1)
            dve.wait_ge(S["f_sq"], i + 1)
            V.tensor_scalar(fst[0:nt, 2 + j:3 + j], fst[0:nt, j:j + 1], 1.0 / D, EPS, ALU.mult, ALU.add).then_inc(S["f_ms"], 1)
            dve.wait_ge(S["f_rs"], i + 1)
            V.scalar_tensor_tensor(fa[j][0:nt, :], fa[j][0:nt, :], fst[0:nt, 4 + j:5 + j], Afb[0:nt, :], ALU.mult, ALU.mult).then_inc(S["f_aff"], 1)

        f_loads = lambda i, j: (i - j) * 16 + 32
        with dve.Fori(0, NTILE // 2) as q:
            for j in range(2):
                final(2 * q + j, j)
        dve.wait_ge(S["smod_in"], 16 * 10)
        chain(V.scalar_tensor_tensor(Afb[0:NS, :], Afb[0:NS, :], 1.0, gfb[0:NS, :], ALU.add, ALU.mult))
        final(NTILE, 0, NS)

    @block.tensor
    def _(pe):
        M = nc.tensor
        tpu, z, xt, ti, kd = Tally(), Tally(), Tally(), Tally(), Tally()
        pe.wait_ge(S["const_in"], 128)
        pe.wait_ge(S["c_ready"], 1)
        for k in range(KD):
            last = M.transpose(ly[:, k * NC:(k + 1) * NC], c9[:, k * P:(k + 1) * P], ident[0:NC, 0:NC])
        last.then_inc(S["prep_pe"], 1)
        pe.wait_ge(S["small_in"], 144)
        M.transpose(ms[:, 0:24], vecs[:], ident[0:24, 0:24])
        for c in range(CH):
            last = M.transpose(ms[:, 32 + c * TAPS:32 + (c + 1) * TAPS], dwr[:, c * P:(c + 1) * P], ident[0:TAPS, 0:TAPS])
        last.then_inc(S["prep_pe"], 1)

        def mod(n):
            pe.wait_ge(S["ada_in"][n % 2], 16 * (n // 2 + 1))
            if n >= 2:
                pe.wait_ge(S["mod_drained"], n - 1)
            for k in range(KD):
                last = M.matmul(zb[n % 2][0:NC, :], cT[:, k, :], big[:, n % 2, k, :], start=(k == 0), stop=(k == KD - 1))
            last.then_inc(S["mod_filled"], 1)

        def rows_T(src, nt, done):
            u = tpu.now
            for h in range(2):
                wait(pe, S["tp_drained"], 2 * u + h - 1)
                for kk in range(4):
                    k = 4 * h + kk
                    last = M.transpose(tp[h][:, kk * P:kk * P + nt], src[0:nt, k * P:(k + 1) * P], ident[0:nt, 0:nt])
                last.then_inc(done, 1)
            tpu.step()

        def xT_(j, nt=P):
            pe.wait_ge(S["xn_ready"], xt.step())
            rows_T(xin[j], nt, S["xt_filled"])

        def zbank():
            wait(pe, S["z_drained"], z.now - 1)
            b = zb[z.n % 2]
            z.step()
            return b

        def pool_mm(p, src, nt):
            for g_ in range(CH):
                b = zbank()
                M.matmul(b[:, 0:nt], w_pool[:, g_, :], src[:, g_, 0:nt], start=True, stop=True).then_inc(S["zp_filled"], 1)

        def w_in_mm():
            order = list(range(CH)) + [c for j in range(CH) for c in (2 * CH + j, CH + j)]
            for m in order:
                b = zbank()
                for k in range(KD):
                    last = M.matmul(b[:, 0:SUP], win[:, k, m * P:(m + 1) * P], hT[:, k, :], start=(k == 0), stop=(k == KD - 1))
                last.then_inc(S["zw_filled"], 1)

        def y_T(i, src, c0, nt=P):
            wait(pe, S["ly_drained"], i)
            for c in range(CH):
                last = M.transpose(ly[0:nt, c * P:(c + 1) * P], src[:, c, c0:c0 + nt], ident[:])
            last.then_inc(S["ly_filled"], 1)

        def yn_T(i, nt=P):
            pe.wait_ge(S["ly_drained"], i + 1)
            b = zbank()
            for c in range(CH):
                last = M.transpose(b[:, c * P:c * P + nt], yn[0:nt, c * P:(c + 1) * P], ident[0:nt, 0:nt])
            last.then_inc(S["zl_filled"], 1)

        def w_out_mm(i, j, zn, nt=P):
            pe.wait_ge(S["z_drained"], zn)
            wait(pe, S["mix_drained"], i)
            for n in range(2):
                for k in range(KD):
                    lhs = mixP[:, k, j * P:j * P + nt] if k < CH else mixC[:, j, k - CH, 0:nt]
                    last = M.matmul(mx[n][0:nt, :], lhs, big[:, n, k, :], start=(k == 0), stop=(k == KD - 1))
            last.then_inc(S["mix_filled"], 1)

        def h_T(i, nt=P):
            pe.wait_ge(S["h2_ready"], i + 1)
            rows_T(h2, nt, S["h_filled"])

        def logits(i, nt=P):
            pe.wait_ge(S["tp_drained"], 2 * tpu.now)
            wait(pe, S["lg_drained"], i)
            wait(pe, S["rk_drained"], kd.now)
            for k in range(KD):
                last = M.matmul(ms[0:nt, 0:NE], h2T[:, k, 0:nt], w_router[:, k, :], start=(k == 0), stop=(k == KD - 1))
            last.then_inc(S["lg_filled"], 1)

        def ranks(i, lg, nt=P):
            pe.wait_ge(S["lg_drained"], lg)
            wait(pe, S["rk_drained"], i)
            pe.wait_ge(S["m_ready"], i + 1)
            wait(pe, S["pairs_ready"], i)
            M.matmul(ms[0:nt, NE:2 * NE], ones[:, 0:nt], Macc[:], start=True, stop=False)
            M.matmul(ms[0:nt, NE:2 * NE], tri[0:nt, 0:nt], Mt[0:nt, :], start=False, stop=True).then_inc(S["rk_filled"], 1)
            kd.step()

        def step(s, has_in, has_next, has_post):
            i = ti.now
            if has_post:
                pe.wait_ge(S["d_ready"], CH * s)
                pool_mm(s - 1, dd, SUP)
            if has_in:
                pe.wait_ge(S["tp_drained"], 2 * tpu.now)
                w_in_mm()
            if has_next:
                xT_(0)
            if has_post:
                pe.wait_ge(S["conv_link"], CH * TAPS * s)
                y_T(i, y, 0)
            if has_next:
                xT_(1)
            if has_post:
                yn_T(i)
                z0 = z.now
                y_T(i + 1, y, P)
                w_out_mm(i, 0, z0)
                yn_T(i + 1)
                w_out_mm(i + 1, 1, z.now)
                h_T(i)
                logits(i)
                h_T(i + 1)
                logits(i + 1)
                ranks(i, i + 2)
                ranks(i + 1, i + 2)
                ti.step(TPS)

        pe.wait_ge(S["prep_act"], 3)
        for n in range(4):
            mod(n)
        pe.wait_ge(S["mod_drained"], 4)
        for m in range(2):
            for k in range(KD):
                src = mrow[:, 2 * m + k // 4, (k % 4) * P:(k % 4 + 1) * P]
                last = M.transpose(tp[0][:, (m * KD + k) * NC:(m * KD + k + 1) * NC], src, ident[0:NC, 0:NC])
        last.then_inc(S["mod1_t"], 1)
        pe.wait_ge(S["aff_ready"], 2)
        for j in range(TPS):
            xT_(j)
        for n in range(4, SBLK):
            mod(n)
        pe.wait_ge(S["mod_drained"], SBLK)
        pe.wait_ge(S["win_in"], 16)
        step(0, True, True, False)
        pe.wait_ge(S["wout_in"], 32)
        step(1, True, True, True)
        with rolled(pe, NSUP - 3, {tpu: 2 * TPS, z: CH + ZC + TPS, xt: TPS, ti: TPS, kd: TPS}) as i:
            step(i + 2, True, True, True)
        step(NSUP - 1, True, False, True)
        step(NSUP, False, False, True)
        xT_(0, NS)
        pe.wait_ge(S["sm_h"], 1)
        b = zbank()
        for m in range(ZC):
            for k in range(KD):
                last = M.matmul(b[:, m * NS:(m + 1) * NS], win[:, k, m * P:(m + 1) * P], hT[:, k, 0:NS], start=(k == 0), stop=(k == KD - 1))
        last.then_inc(S["zw_filled"], 1)
        pe.wait_ge(S["state_in"], 48)
        for i, nr in enumerate((NS * POOLB, 4 * CONVB, 4 * CONVB)):
            b = zbank()
            for c in range(CH):
                last = M.transpose(b[:, c * P:c * P + nr], strow[i][0:nr, c * P:(c + 1) * P], ident[0:nr, 0:nr])
            last.then_inc(S["edge_tp"], 1)
        edges = [(u_buf, 0, POOLB), (a_buf, SUP, CONVB), (usm, 0, NS), (asm, 0, NS)]
        pe.wait_ge(S["d_ready"], CH * NSUP)
        pe.wait_ge(S["sm_y"], 1)
        for i, (t, c0, n) in enumerate(edges):
            if i < 2:
                wait(pe, S["z_drained"], z.now - 1)
            else:
                pe.wait_ge(S["edge_ready"], i - 1)
            b = zb[z.n % 2]
            z.step()
            for c in range(CH):
                last = M.transpose(b[0:n, c * P:(c + 1) * P], t[:, c, c0:c0 + n], ident[:])
            last.then_inc(S["edge_tp"], 1)
        pe.wait_ge(S["edge_ready"], 4)
        z.step(-4)
        pool_mm(NSUP, dsm, NS)
        y_T(NTILE, ysm, 0, NS)
        yn_T(NTILE, NS)
        w_out_mm(NTILE, 0, z.now, NS)
        h_T(NTILE, NS)
        logits(NTILE, NS)
        ranks(NTILE, NTILE + 1, NS)
        pe.wait_ge(S["pairs_ready"], NTILE + 1)
        M.matmul(ms[0:NE, 0:1], Macc[:], ones[:, 0:1], start=True, stop=True).then_inc(S["cnt_filled"], 1)
        pe.wait_ge(S["cnt_ready"], 1)
        M.matmul(ms[0:NE, 0:1], uinc[:], nb[:], start=True, stop=True)
        M.matmul(ms[0:1, NE:2 * NE], nb[:], uinc[:], start=True, stop=True).then_inc(S["cnt_filled"], 1)
        pe.wait_ge(S["cnt_ready"], 2)
        M.matmul(ms[0:1, 0:NBT], ones[0:NE, 0:1], amat[:], start=True, stop=True)
        M.matmul(zb[0][0:1, 0:NBT], nb[:], amat[:], start=True, stop=True).then_inc(S["cnt_filled"], 1)
        if stop < 2:
            return

        pe.wait_ge(S["tables_ready"], 1)
        nblk = pe.value_load(ctab[0:1, NE:NE + 1], min_val=EB, max_val=MAXB)
        wg3 = wgu[:].rearrange("p s k g n -> p (s k) (g n)")
        wd3 = wd[:].rearrange("p s k n -> p (s k) n")

        def gx(b, j, n):
            pe.wait_ge(S["gath"][j], n)
            for h in range(2):
                if h == 0:
                    wait(pe, S["gx_act"], b)
                else:
                    wait(pe, S["gx_dve"], b)
                for kk in range(4):
                    k = 4 * h + kk
                    last = M.transpose(tp[h][:, kk * P:(kk + 1) * P], xg[j][:, k * P:(k + 1) * P], ident[:])
                last.then_inc(S["gx_filled"], 1)

        def gate_up(b, j):
            o = pe.value_load(btab[0:1, 1, ds(b, 1)], min_val=0, max_val=NE)
            sl = pe.value_load(btab[0:1, 2, ds(b, 1)], min_val=0, max_val=1)
            pe.wait_ge(S["w_landed"], o * 48 + 48)
            pe.wait_ge(S["gx_act"], b + 1)
            pe.wait_ge(S["gx_dve"], b + 1)
            wait(pe, S["hh_ready"], b - 1)
            for k in range(KD):
                rhs = wg3[:, ds(sl * KD + k, 1), :].rearrange("p s n -> p (s n)")
                last = M.matmul(zb[j][:], xT[:, k, :], rhs, start=(k == 0), stop=(k == KD - 1))
            last.then_inc(S["gu_filled"], 1)

        def down(b):
            sl = pe.value_load(btab[0:1, 2, ds(b, 1)], min_val=0, max_val=1)
            pe.wait_ge(S["ht_drained"], b + 1)
            wait(pe, S["o_act"], b)
            wait(pe, S["o_dve"], b)
            for n in range(2):
                for k in range(KE):
                    rhs = wd3[:, ds(sl * KE + k, 1), n * 512:(n + 1) * 512].rearrange("p s n -> p (s n)")
                    last = M.matmul(mx[n][:], hhT[:, k, :], rhs, start=(k == 0), stop=(k == KE - 1))
            last.then_inc(S["o_filled"], 1)

        def ht(b):
            pe.wait_ge(S["hh_ready"], b + 1)
            for k in range(KE):
                last = M.transpose(ly[:, k * P:(k + 1) * P], hh[:, k * P:(k + 1) * P], ident[:])
            last.then_inc(S["ht_filled"], 1)

        gx(0, 0, 16)
        gate_up(0, 0)
        gx(1, 1, 16)
        ht(0)

        def turn(q):
            for h in range(2):
                b, j = 2 * q + 1 + h, (1 + h) % 2
                gate_up(b, j)
                gx(b + 1, 1 - j, 16 * q + 32)
                down(b - 1)
                ht(b)

        turn(0)
        with pe.Fori(0, (MAXB - 1) // 2) as q:
            with pe.If(2 * q + 2 < nblk):
                turn(q + 1)
        turns = (nblk + 1) // 2
        pe.wait_ge(S["gath"][0], turns * 16 + 32)
        pe.wait_ge(S["gath"][1], turns * 16 + 16)
    ctx.close()


_INS = ["x_prompt", "x_sample", "state_pool", "state_conv", "c_prompt", "c_sample", "w_ada", "b_ada", "g_mix", "w_in",
        "w_pool", "pool_scale", "w_dw", "b_dw", "ln_g", "ln_b", "w_out", "g_ffn", "w_router", "b_router", "w_gate",
        "w_up", "w_down", "ws_gate", "ws_up", "ws_down", "w_ada_final", "b_ada_final", "g_final"]
_OUTS = [(1, SEQ, D), (NS, 1, D), (1, 1, POOLB, PW), (1, 1, CONVB, PW), (1, NS, POOLB, PW), (1, NS, CONVB, PW)]


def constants():
    import numpy as np

    f = np.float32
    t = np.arange(16)
    fix = np.stack([w / np.minimum(w, t + 1) for w in (2, 4, 8, 16)]).astype(f)
    b = np.arange(NBT)
    return {
        "ident": np.eye(P, dtype=f),
        "tri": np.triu(np.ones((P, P), f), 1),
        "ones": np.ones((P, P), f),
        "poolfix": np.ascontiguousarray(np.broadcast_to(fix, (P, CH, 16))),
        "iota64": np.ascontiguousarray(np.broadcast_to(np.arange(NE, dtype=f), (P, NE))),
        "base17": np.ascontiguousarray(np.broadcast_to(np.arange(NE, dtype=f) * EB, (P, NE))),
        "thr": np.ascontiguousarray(np.broadcast_to(np.array([-1.0] + [P * m for m in range(1, EB)], f), (NE, EB))),
        "uinc": np.triu(np.ones((NE, NE), f)),
        "brow": np.stack([np.where(b < EB, SHCOL + b, b - EB), b >= EB]).astype(f)[None],
        "biota": np.ascontiguousarray(np.broadcast_to(b.astype(f), (NE, NBT))),
    }


def kernel(**inputs):
    import numpy as np
    import concourse.bacc as bacc
    from concourse.bass_utils import run_bass_kernel_spmd as run

    nc = bacc.Bacc("TRN2", target_bir_lowering=False, num_devices=1)
    arrays, a, const = {}, {}, {}
    for name in _INS:
        arrays[f"in_{name}"] = np.ascontiguousarray(inputs[name])
        a[name] = nc.dram_tensor(f"in_{name}", arrays[f"in_{name}"].shape, F32, kind="ExternalInput").ap()
    for name, v in constants().items():
        arrays[f"const_{name}"] = v
        const[name] = nc.dram_tensor(f"const_{name}", v.shape, F32, kind="ExternalInput").ap()
    out = [nc.dram_tensor(f"out_{i}", s, F32, kind="ExternalOutput").ap() for i, s in enumerate(_OUTS)]
    program(nc, a, const, out)
    r = run(nc, [arrays], core_ids=[0])
    return tuple(r.results[0][f"out_{i}"] for i in range(len(_OUTS)))
```

```python
from contextlib import ExitStack, contextmanager

import concourse.bass as bass
from concourse import mybir

F32 = mybir.dt.float32
F32R = mybir.dt.float32r
BF16 = mybir.dt.bfloat16
I32 = mybir.dt.int32
U32 = mybir.dt.uint32
ACT = mybir.ActivationFunctionType
ALU = mybir.AluOpType
AX = mybir.AxisListType
ds = bass.ds

P = 128
D = 1024
KD = D // P
SEQ = 2048
NS = 8
T = SEQ + NS
TROWS = 18 * P
NC = NS + 1
PW = 512
CH = PW // P
DIN = 3 * PW
ZC = DIN // P
POOLB, CONVB, TAPS = 15, 30, 31
NE, NG, TOPG, TOPK = 64, 8, 4, 8
DE = 256
KE = DE // P
SCALE = 2.5
EPS = 1e-6
BIG = 3.0e38
SUP = 256
TPS = SUP // P
NSUP = SEQ // SUP
NTILE = SEQ // P
EB = -(-T // P)
NCOL = NE * EB + EB + 1
SHCOL = NE * EB
PADCOL = NCOL - 1
MAXB = EB + (T * TOPK) // P + NE
NBT = MAXB + 7
NORD = NE + 1
UG, UD = KD, KE * D // 512
UW = UG + UD
FB = 4
SBLK = 16
CREP = NE * EB // 16


class Tally:

    def __init__(self):
        self.base, self.n = 0, 0

    @property
    def now(self):
        return self.base + self.n

    def step(self, k=1):
        self.n += k
        return self.now


@contextmanager
def rolled(eng, count, per):
    starts = {t: t.now for t in per}
    with eng.Fori(0, count) as i:
        for t, k in per.items():
            t.base, t.n = starts[t] + i * k, 0
        yield i
        bad = [(t.n, k) for t, k in per.items() if t.n != k]
        assert not bad, bad
    for t, k in per.items():
        t.base, t.n = starts[t] + count * k, 0


class Goal:

    def __init__(self, eng, name, start, step):
        self.eng, self.by, self.reg = eng, step, eng.alloc_register(name)
        eng.reg_mov(self.reg, start)

    def wait(self, sem):
        self.eng.wait_ge(sem, self.reg)
        self.eng.reg_add(self.reg, self.reg, self.by)


def wait(eng, sem, value):
    if isinstance(value, int) and value <= 0:
        return
    eng.wait_ge(sem, value)


def program(nc, a, const, out):
    ctx = ExitStack()

    def sem(name):
        return ctx.enter_context(nc.semaphore(name))

    def sb(name, shape, dt=F32, stack=ctx):
        return stack.enter_context(nc.sbuf_tensor("b_" + name, shape, dt))

    def dram(name, shape, dt=F32):
        return nc.dram_tensor(name, shape, dt, kind="Internal").ap()

    def bank(name):
        return ctx.enter_context(nc.psum_tensor(name, [P, 512], F32))

    mod_d = dram("mod_d", (NC, 8 * D))
    x1_d = dram("x1_d", (T, D))
    hf_d = dram("hf_d", (T + P, D))
    acc_d = dram("acc_d", (TROWS, D))
    list_d = dram("list_d", (P * NCOL, 2), I32)
    x_p = a["x_prompt"].rearrange("b t d -> (b t) d")
    x_s = a["x_sample"].rearrange("b t d -> (b t) d")

    tp = [bank("tp0"), bank("tp1")]
    zb = [bank("zb0"), bank("zb1")]
    ly = bank("ly")
    mx = [bank("mx0"), bank("mx1")]
    ms = bank("ms")

    ident = sb("ident", [P, P]); ones = sb("ones", [P, P]); half = sb("half", [P, 1])
    btab = sb("btab", [1, 5, NBT], I32)
    ctab = sb("ctab", [1, NORD], I32)

    win = sb("win", [P, KD, DIN])
    stage = win[:].rearrange("p k n -> p (k n)").rearrange("p (u n) -> p u n", n=512)

    names = """const_in c_in small_in win_in wout_in state_in bc_in zero_st init_st edge_st xres_in x1_st h2_st smod_in
        dve_link pool_link csig prep_pe prep_act c_ready mod_filled mod_drained mod1_t aff_ready
        xt_filled h_filled tp_drained zp_filled zw_filled zl_filled z_drained ly_filled ly_drained
        mix_filled mix_drained lg_filled lg_drained rk_filled rk_drained xsq xms xrs xn_ready lnv lnr
        x1_ready x1_sq x1_ms x1_rs h2_ready a_ready a_taken d_ready conv_link m_ready pairs_ready
        pool_const dve_const sm_h sm_y edge_tp edge_ready
        cnt_filled cnt_ready row_in table_in tables_ready w_landed w_hi w_lo scatb gu_filled sg_ready hh_ready
        gx_filled gx_hi gx_lo ht_filled ht_hi ht_lo o_filled o_act o_dve f_gated f_sum f_sq f_ms f_rs f_aff f_y""".split()
    S = {n: sem(n) for n in names}
    for n in ("ada_in", "adab_in", "xin_in", "scat", "gath"):
        S[n] = [sem(f"{n}0"), sem(f"{n}1")]
    for n in ("fin_in", "fin_st"):
        S[n] = [sem(f"{n}{i}") for i in range(FB)]
    S["modrow_st"] = [sem(f"modrow_st{i}") for i in range(4)]

    front = ExitStack()

    def f(name, shape, dt=F32):
        return sb(name, shape, dt, front)

    tri = f("tri", [P, P])
    poolfix = f("poolfix", [P, CH, 16]); iota64 = f("iota64", [P, NE]); base17 = f("base17", [P, NE])
    thr = f("thr", [NE, EB]); uinc = f("uinc", [NE, NE])
    vecs = f("vecs", [24, P]); vecT = f("vecT", [P, 24]); dwr = f("dwr", [P, PW]); wdw = f("wdw", [P, CH, TAPS])
    router_b = f("router_b", [P, NE]); w_router = f("w_router", [P, KD, NE]); w_pool = f("w_pool", [P, CH, P])
    A1T = f("A1T", [P, KD, NC]); B1T = f("B1T", [P, KD, NC])
    g1b = f("g1b", [P, D]); A2b = f("A2b", [P, D]); B2b = f("B2b", [P, D])
    big = f("big", [P, 2, KD, 512])
    hT = f("hT", [P, KD, SUP])
    av = f("av", [P, CH, SUP]); a_buf = f("a_buf", [P, CH, CONVB + SUP]); u_buf = f("u_buf", [P, CH, POOLB + SUP])
    y = f("y", [P, CH, SUP]); dd = f("dd", [P, CH, SUP]); mixP = f("mixP", [P, CH, SUP]); mixC = f("mixC", [P, TPS, CH, P])
    sgt = f("sgt", [P, 2, SUP]); vv = f("vv", [P, 2, SUP]); pa = f("pa", [P, 2, POOLB + SUP])
    xin = [f("xin0", [P, D]), f("xin1", [P, D])]; xres = f("xres", [P, D]); x1b = f("x1b", [P, D]); h2 = f("h2", [P, D])
    h2T = f("h2T", [P, KD, P]); yn = f("yn", [P, PW]); junk = f("junk", [P, D], BF16)
    st = f("st", [P, 16]); bn6 = f("bn6", [P, 6]); bn2 = f("bn2", [P, 2])
    sg_r = f("sg_r", [P, TPS, NE]); sel = f("sel", [P, TPS, NE]); m8 = f("m8", [P, TPS * NG, 8])
    gsc = f("gsc", [P, TPS, NG]); gm = f("gm", [P, TPS, 8]); gi = f("gi", [P, TPS, 8], U32); gif = f("gif", [P, TPS, 8])
    oh4 = f("oh4", [P, TPS, NG, TOPG]); gmask = f("gmask", [P, TPS * NG]); pen = f("pen", [P, TPS * NG])
    oh = f("oh", [P, TPS, TOPK, NE]); Mt = f("Mt", [P, TPS, NE]); Macc = f("Macc", [P, NE]); prod = f("prod", [P, TPS, TOPK, NE])
    wk = f("wk", [P, TPS, TOPK]); wsum = f("wsum", [P, 2, TPS])
    ri = f("ri", [P, 3, TPS, NE], I32); dst = f("dst", [P, TPS, NE]); dk = f("dk", [P, TPS, TOPK])
    rows = f("rows", [P, TPS, TOPK], I32); pairs = f("pairs", [P, TPS, TOPK, 2], I32); tokid = f("tokid", [P, TPS], I32)
    usm = f("usm", [P, CH, NS]); asm = f("asm", [P, CH, NS]); gsm = f("gsm", [P, CH, NS])
    ysm = f("ysm", [P, CH, NS]); dsm = f("dsm", [P, CH, NS]); xsT = f("xsT", [P, KD, NS])
    cnt = f("cnt", [NE, 1]); nb = f("nb", [NE, 1]); ccum = f("ccum", [NE, 1]); nbt = f("nbt", [NE, EB])
    early = ExitStack()
    c9, cs9 = (t[0:NC].rearrange("p c t -> p (c t)") for t in (dd, y))
    cT = sb("cT", [P, KD, NC], F32, early)
    mrow = sb("mrow", [NC, 4, 512], F32, early); mbias = sb("mbias", [NC, 2, 512], F32, early)
    lpad = sb("lpad", [P, CREP, 2], I32, early); lsh = sb("lsh", [P, EB + 1, 2], I32, early)
    early.close()
    late = ExitStack()
    full_c = sb("full_c", [P, CH, NS, TAPS], F32, late); full_p = sb("full_p", [P, CH, NS, POOLB + 1], F32, late)
    strow = [dwr, sb("strow1", [P, PW], F32, late), sb("strow2", [P, PW], F32, late)]
    xs = sb("xs", [NS, D], F32, late)
    edge = hT[:].rearrange("p k t -> p (k t)").rearrange("p (o c) -> p o c", o=4)
    late.close()
    front.close()

    by_x, by_w = xin[0][:], big[:].rearrange("p h k n -> p (h k n)")
    brow = by_x[0:1, 0:2 * NBT].rearrange("p (r b) -> p r b", r=2); biota = by_x[0:NE, 2 * NBT:3 * NBT]
    tabf = by_w[0:1, 0:7 * NBT].rearrange("p (r b) -> p r b", r=7); amat = by_w[0:NE, 7 * NBT:8 * NBT]

    moe = ExitStack()

    def g(name, shape, dt=F32):
        return sb(name, shape, dt, moe)

    lt = g("lt", [P, NCOL, 2], I32)
    ltf = lt[:].rearrange("p c w -> p (c w)").bitcast(F32)
    xg = [g("xg0", [P, D]), g("xg1", [P, D])]
    xh = g("xh", [P, KD, P], F32R); xl = g("xl", [P, KD, P], F32R)
    sgx = [g("sgx0", [P, DE]), g("sgx1", [P, DE])]; hh = g("hh", [P, DE]); hth = g("hth", [P, KE, P], F32R); htl = g("htl", [P, KE, P], F32R)
    ob = [g("ob0", [P, D]), g("ob1", [P, D])]
    gidx = [g("gidx0", [P, 1], I32), g("gidx1", [P, 1], I32)]; sidx = [g("sidx0", [P, 1], I32), g("sidx1", [P, 1], I32)]
    g2b, Bfb, Afb = (g(n, [P, D]) for n in ("g2b", "Bfb", "Afb"))
    heavy = ExitStack()
    wh = sb("wh", [P, 2 * UW, 512], F32R, heavy)
    wl = sb("wl", [P, 2 * UW, 512], F32R, heavy)
    heavy.close()
    fin = ExitStack()
    fa, fx, fy = ([sb(f"{n}{i}", [P, D], F32, fin) for i in range(FB)] for n in ("fa", "fx", "fy"))
    gfb = sb("gfb", [P, D], F32, fin)
    g2s, Bfs, Afs = (sb(n, [NS, D], F32, fin) for n in ("g2s", "Bfs", "Afs"))
    fjunk = sb("fjunk", [P, D], BF16, fin); fst = sb("fst", [P, 3 * FB], F32, fin)
    fin.close()
    moe.close()

    w_ada = a["w_ada"][0].rearrange("(k p) n -> p k n", p=P)
    w_fin = a["w_ada_final"].rearrange("(k p) n -> p k n", p=P)
    b_fin = a["b_ada_final"].rearrange("(o n) -> o n", o=1)
    ada_cols = [(w_ada, a["b_ada"], n * 512) for n in range(12)] + [(w_fin, b_fin, n * 512) for n in range(4)]
    mod_row = lambda m, r0, r1: mod_d[r0:r1, m * D:(m + 1) * D]
    MOD_G1, MOD_SH2, MOD_SC2, MOD_G2, MOD_SHF, MOD_SCF = 2, 3, 4, 5, 6, 7

    block = ctx.enter_context(nc.Block())


    def front_stored(eng):
        eng.wait_ge(S["edge_st"], 96)
        eng.wait_ge(S["x1_st"], 16 * (NTILE + 1))
        eng.wait_ge(S["h2_st"], 16 * (NTILE + 1))

    @block.sync
    def _(sp):
        for t, name in ((ident, "ident"), (tri, "tri"), (ones, "ones"), (poolfix, "poolfix"), (iota64, "iota64"),
                        (base17, "base17"), (thr, "thr"), (uinc, "uinc")):
            sp.dma_start(t[:], const[name]).then_inc(S["const_in"], 16)
        sp.dma_start(c9[0:NS, :], a["c_sample"]).then_inc(S["c_in"], 16)
        sp.dma_start(c9[NS:NC, :], a["c_prompt"]).then_inc(S["c_in"], 16)
        for i, name in enumerate(("b_dw", "ln_g", "ln_b", "pool_scale")):
            sp.dma_start(vecs[4 * i:4 * i + 4, :], a[name].rearrange("o (r p) -> (o r) p", p=P)).then_inc(S["small_in"], 16)
        sp.dma_start(vecs[16:24, :], a["g_mix"].rearrange("o (r p) -> (o r) p", p=P)).then_inc(S["small_in"], 16)
        sp.dma_start(dwr[0:TAPS, :], a["w_dw"][0]).then_inc(S["small_in"], 16)
        sp.dma_start(router_b[:], a["b_router"].to_broadcast([P, NE])).then_inc(S["small_in"], 16)
        sp.dma_start(w_router[:], a["w_router"][0].rearrange("(k p) n -> p k n", p=P)).then_inc(S["small_in"], 16)
        sp.dma_start(w_pool[:], a["w_pool"][0].rearrange("g c d -> c g d")).then_inc(S["small_in"], 16)

        def load_x(s, j):
            sp.dma_start(xin[j][:], x_p[ds(s * SUP + j * P, P), :]).then_inc(S["xin_in"][j], 16)

        def reload_x(s):
            for j in range(TPS):
                sp.wait_ge(S["xt_filled"], 2 * TPS * (s - 1) + 2 * j + 2)
                load_x(s, j)

        shared = [a["ws_gate"][0], a["ws_up"][0], a["ws_down"][0]]
        stage_gu = stage.rearrange("p (s u) (g n) -> p s u g n", s=2, g=2)
        stage_d = stage.rearrange("p (s u) n -> p s (u n)", s=2)[:, :, UG * 512:]

        def load_w(set_, gate, up, down):
            sp.dma_start(stage_gu[:, set_, 0:UG, 0, :], gate.rearrange("(k p) n -> p k n", p=P)).then_inc(S["w_landed"], 16)
            sp.dma_start(stage_gu[:, set_, 0:UG, 1, :], up.rearrange("(k p) n -> p k n", p=P)).then_inc(S["w_landed"], 16)
            sp.dma_start(stage_d[:, set_].rearrange("p (k n) -> p k n", k=KE), down.rearrange("(k p) n -> p k n", p=P)).then_inc(S["w_landed"], 16)

        def expert(e):
            return [a[n][0].rearrange("e d n -> (e d) n")[ds(e * r, r), :] for n, r in (("w_gate", D), ("w_up", D), ("w_down", DE))]

        for n in range(SBLK):
            w, b, c0 = ada_cols[n]
            if n >= 2:
                sp.wait_ge(S["mod_filled"], n - 1)
            sp.dma_start(big[:, n % 2, :, :], w[:, :, c0:c0 + 512]).then_inc(S["ada_in"][n % 2], 16)
            if n >= 2:
                sp.wait_ge(S["mod_drained"], n - 1)
            sp.dma_start(mbias[:, n % 2, :], b[0:1, c0:c0 + 512].to_broadcast([NC, 512])).then_inc(S["adab_in"][n % 2], 16)
            if n >= 2:
                sp.dma_start(mod_d[:, (n - 2) * 512:(n - 1) * 512], mrow[:, (n - 2) % 4, :]).then_inc(S["modrow_st"][(n - 2) % 4], 16)
            if n == 1:
                load_x(0, 0)
                load_x(0, 1)
            if 4 <= n < 4 + KD:
                sp.dma_start(win[:, n - 4, :], a["w_in"][0, (n - 4) * P:(n - 3) * P, :]).then_inc(S["win_in"], 16)
            if n == 8:
                reload_x(1)
            if n == 5:
                sp.wait_ge(S["pool_const"], 6)
                sp.dma_start(hf_d[T:T + P, :], x1b[:]).then_inc(S["zero_st"], 16)
                lists = list_d.rearrange("(p c) w -> p (c w)", p=P)
                sp.dma_start(lists[:, 0:2 * SHCOL].rearrange("p (r c) -> p r c", r=16),
                             lpad[:].rearrange("p c w -> p (c w)").unsqueeze(1).to_broadcast([P, 16, 2 * CREP])).then_inc(S["init_st"], 16)
                sp.dma_start(lists[:, 2 * SHCOL:2 * NCOL], lsh[:].rearrange("p c w -> p (c w)")).then_inc(S["init_st"], 16)
        for n in (SBLK - 2, SBLK - 1):
            sp.wait_ge(S["mod_drained"], n + 1)
            sp.dma_start(mod_d[:, n * 512:(n + 1) * 512], mrow[:, n % 4, :]).then_inc(S["modrow_st"][n % 4], 16)
        sp.wait_ge(S["mod_filled"], SBLK)
        for n in range(2):
            sp.dma_start(big[:, n, :, :], a["w_out"][0].rearrange("(k p) n -> p k n", p=P)[:, :, n * 512:(n + 1) * 512]).then_inc(S["wout_in"], 16)
        for q in S["modrow_st"]:
            sp.wait_ge(q, 4 * SBLK)
        sp.dma_start(g1b[:], mod_row(MOD_G1, NS, NC).to_broadcast([P, D])).then_inc(S["bc_in"], 16)
        sp.dma_start(B2b[:], mod_row(MOD_SH2, NS, NC).to_broadcast([P, D])).then_inc(S["bc_in"], 16)
        sp.dma_start(A2b[:], mod_row(MOD_SC2, NS, NC).to_broadcast([P, D])).then_inc(S["bc_in"], 16)
        sp.dma_start(h2[:], a["g_ffn"].to_broadcast([P, D])).then_inc(S["bc_in"], 16)

        sp.dma_start(acc_d.rearrange("(t p) n -> p t n", p=P),
                     x1b[:, :].unsqueeze(1).to_broadcast([P, TROWS // P, D])).then_inc(S["zero_st"], 16)
        sp.wait_ge(S["init_st"], 32)
        sp.wait_ge(S["mod1_t"], 1)
        sp.dma_start(xs[:], x_s).then_inc(S["state_in"], 16)
        sp.dma_start(strow[0][0:NS * POOLB, :], a["state_pool"][0].rearrange("b t c -> (b t) c")).then_inc(S["state_in"], 16)
        conv_rows = a["state_conv"][0].rearrange("b t c -> (b t) c")
        for h in range(2):
            sp.dma_start(strow[1 + h][0:4 * CONVB, :], conv_rows[h * 4 * CONVB:(h + 1) * 4 * CONVB, :]).then_inc(S["state_in"], 16)
        sp.dma_start(out[4][0, :, 0:POOLB - 1, :], a["state_pool"][0, :, 1:POOLB, :]).then_inc(S["edge_st"], 16)
        sp.dma_start(out[5][0, :, 0:CONVB - 1, :], a["state_conv"][0, :, 1:CONVB, :]).then_inc(S["edge_st"], 16)

        tile = Tally()

        def tile_io(src, nt):
            i = tile.now
            wait(sp, S["x1_ready"], i)
            sp.dma_start(xres[0:nt, :], src).then_inc(S["xres_in"], 16)
            sp.wait_ge(S["x1_ready"], i + 1)
            sp.dma_start(x1_d[ds(i * P, nt), :], x1b[0:nt, :]).then_inc(S["x1_st"], 16)
            sp.wait_ge(S["h2_ready"], i + 1)
            sp.dma_start(hf_d[ds(i * P, nt), :], h2[0:nt, :]).then_inc(S["h2_st"], 16)
            tile.step()

        def step(s, has_next, has_post):
            if has_next:
                reload_x(s + 2)
            if has_post:
                for j in range(TPS):
                    tile_io(x_p[ds(tile.now * P, P), :], P)

        step(0, True, False)
        step(1, True, True)
        with rolled(sp, NSUP - 4, {tile: TPS}) as i:
            step(i + 2, True, True)
        step(NSUP - 2, False, True)
        step(NSUP - 1, False, True)
        sp.wait_ge(S["zw_filled"], NSUP * ZC + 1)
        load_w(0, *shared)
        sp.wait_ge(S["w_landed"], 48)
        load_w(1, *expert(0))
        step(NSUP, False, True)
        sp.wait_ge(S["xt_filled"], 2 * NTILE)
        sp.dma_start(brow, const["brow"]).then_inc(S["row_in"], 16)
        sp.dma_start(biota, const["biota"]).then_inc(S["row_in"], 16)
        sp.dma_start(xin[1][0:NS, :], a["g_ffn"].to_broadcast([NS, D])).then_inc(S["xin_in"][1], 16)
        sp.wait_ge(S["h2_ready"], NTILE)
        for m, t in ((MOD_G1, g1b), (MOD_SH2, B2b), (MOD_SC2, A2b)):
            sp.dma_start(t[0:NS, :], mod_row(m, 0, NS)).then_inc(S["smod_in"], 16)
        tile_io(x_s, NS)
        sp.wait_ge(S["edge_ready"], 4)
        sp.dma_start(out[2][0, 0], edge[0:POOLB, 0, :]).then_inc(S["edge_st"], 16)
        sp.dma_start(out[3][0, 0], edge[0:CONVB, 1, :]).then_inc(S["edge_st"], 16)
        sp.dma_start(out[4][0, :, POOLB - 1, :], edge[0:NS, 2, :]).then_inc(S["edge_st"], 16)
        sp.dma_start(out[5][0, :, CONVB - 1, :], edge[0:NS, 3, :]).then_inc(S["edge_st"], 16)
        front_stored(sp)
        sp.wait_ge(S["zero_st"], 32)
        sp.wait_ge(S["scat"][0], 16 * TOPK * (NSUP + 1))
        sp.wait_ge(S["scat"][1], 16 * TOPK * NSUP)
        sp.wait_ge(S["cnt_ready"], 1)
        sp.wait_ge(S["cnt_filled"], 2)
        sp.dma_start(lt[:].rearrange("p c w -> p (c w)"), list_d.rearrange("(p c) w -> p (c w)", p=P)).then_inc(S["table_in"], 16)

        def next_w(n, set_):
            sp.wait_ge(S["w_lo"], UW * (n - 1))
            sp.wait_ge(S["w_landed"], 48 * n)
            load_w(set_, *expert(n - 1))

        sp.wait_ge(S["tables_ready"], 1)
        for m, t in ((MOD_G2, g2b), (MOD_SHF, Bfb), (MOD_SCF, Afb)):
            sp.dma_start(t[:], mod_row(m, NS, NC).to_broadcast([P, D])).then_inc(S["smod_in"], 16)
        next_w(2, 0)
        with sp.Fori(0, (NORD - 3) // 2) as q:
            next_w(2 * q + 3, 1)
            next_w(2 * q + 4, 0)
        sp.wait_ge(S["w_landed"], 48 * NORD)

        turns = (sp.value_load(ctab[0:1, NE:NE + 1], min_val=EB, max_val=MAXB) + 1) // 2
        sp.wait_ge(S["scatb"], turns * 32)
        sp.dma_start(gfb[:], a["g_final"].rearrange("(o n) -> o n", o=1).to_broadcast([P, D])).then_inc(S["smod_in"], 16)
        for m, t in ((MOD_G2, g2s), (MOD_SHF, Bfs), (MOD_SCF, Afs)):
            sp.dma_start(t[:], mod_row(m, 0, NS)).then_inc(S["smod_in"], 16)

        def load_f(i, j, nt=P):
            sp.dma_start(fa[j][0:nt, :], acc_d[ds(i * P, nt), :]).then_inc(S["fin_in"][j], 16)
            sp.dma_start(fx[j][0:nt, :], x1_d[ds(i * P, nt), :]).then_inc(S["fin_in"][j], 16)

        y_p = out[0].rearrange("b t d -> (b t) d")

        def store_f(i, j):
            sp.wait_ge(S["f_y"], i + 1)
            sp.dma_start(y_p[ds(i * P, P), :], fy[j][:]).then_inc(S["fin_st"][j], 16)

        for j in range(FB):
            load_f(j, j)
        with sp.Fori(0, NTILE // FB - 1) as q:
            for j in range(FB):
                store_f(FB * q + j, j)
                load_f(FB * q + j + FB, j)
        for j in range(FB):
            store_f(NTILE - FB + j, j)
            if j == 0:
                load_f(NTILE, 0, NS)
        sp.wait_ge(S["f_y"], NTILE + 1)
        sp.dma_start(out[1].rearrange("b t d -> (b t) d"), fy[0][0:NS, :]).then_inc(S["fin_st"][0], 16)
        for j in range(FB):
            sp.wait_ge(S["fin_st"][j], 16 * (NTILE // FB + (j == 0)))

    @block.gpsimd
    def _(pool):
        linked = Goal(pool, "pool_linked", 1, 1)
        routed = Goal(pool, "pool_routed", 1, 1)
        added = Goal(pool, "pool_added", 32, 16)

        def chain(ins):
            ins.then_inc(S["pool_link"], 1)
            linked.wait(S["pool_link"])

        G = nc.gpsimd
        G.iota(lpad[:, :, 0], [[0, CREP]], base=T, channel_multiplier=1).then_inc(S["pool_const"], 1)
        G.memset(lpad[:, :, 1], 0).then_inc(S["pool_const"], 1)
        G.iota(lsh[:, :, 0], [[P, EB + 1]], base=0, channel_multiplier=1).then_inc(S["pool_const"], 1)
        pool.wait_ge(S["pool_const"], 3)
        G.iota(lsh[:, EB:EB + 1, 0], [[0, 1]], base=T, channel_multiplier=1).then_inc(S["pool_const"], 1)
        G.memset(lsh[:, :, 1].bitcast(F32), 1.0).then_inc(S["pool_const"], 1)
        G.memset(x1b[:], 0.0).then_inc(S["pool_const"], 1)
        G.memset(half[:], -0.5).then_inc(S["pool_const"], 1)
        G.memset(u_buf[:, :, 0:POOLB], 0.0).then_inc(S["pool_const"], 1)
        G.iota(tokid[:], [[P, TPS]], base=-SUP, channel_multiplier=1).then_inc(S["pool_const"], 1)
        pool.wait_ge(S["pool_const"], 9)

        z, xt, lt_i = Tally(), Tally(), Tally()

        def power(src, dst_, ready, value, done, nt=P):
            pool.wait_ge(ready, value)
            G.tensor_tensor(dst_[0:nt], src[0:nt], half[0:nt, :], ALU.pow).then_inc(done, 1)

        def diff(s, g_, first, post):
            w = 2 << g_
            zu = z.now + (CH if post else 0) + g_
            pool.wait_ge(S["z_drained"], zu + 1)
            cur, n = u_buf[:, g_, :], POOLB + SUP
            for lev in range(g_ + 1):
                sh_ = 1 << lev
                o = pa[:, lev % 2, 0:n - sh_]
                chain(G.tensor_tensor(o, cur[:, sh_:n], cur[:, 0:n - sh_], ALU.add))
                cur, n = pa[:, lev % 2, :], n - sh_
            mean = pa[:, (g_ + 1) % 2, 0:SUP]
            chain(G.tensor_scalar(mean, cur[:, 16 - w:16 - w + SUP], 1.0 / w, None, ALU.mult))
            if first:
                chain(G.tensor_tensor(mean[:, 0:16], mean[:, 0:16], poolfix[:, g_, :], ALU.mult))
            if post:
                pool.wait_ge(S["zp_filled"], CH * (s - 1) + g_ + 1)
            chain(G.tensor_tensor(dd[:, g_, :], mean, u_buf[:, g_, POOLB:POOLB + SUP], ALU.subtract))
            G.tensor_copy(u_buf[:, g_, 0:POOLB], u_buf[:, g_, SUP:SUP + POOLB]).then_inc(S["d_ready"], 1)

        def amul(s, j, post):
            zv = z.now + (CH if post else 0) + CH + 2 * j + 1
            pool.wait_ge(S["z_drained"], zv + 1)
            if post:
                pool.wait_ge(S["a_taken"], s)
            G.tensor_tensor(av[:, j, :], sgt[:, j % 2, :], vv[:, j % 2, :], ALU.mult).then_inc(S["a_ready"], 1)

        def scatter(s, tiles=TPS, nt=P):
            if isinstance(s, int):
                pool.wait_ge(S["pairs_ready"], s + 1)
            else:
                routed.wait(S["pairs_ready"])
            for j in range(tiles):
                for k in range(TOPK):
                    G.indirect_dma_start(list_d, bass.IndirectOffsetOnAxis(ap=rows[0:nt, j, k:k + 1], axis=0),
                                         pairs[0:nt, j, k, :], None).then_inc(S["scat"][j], 16)

        def step(s, has_in, has_next, has_post, has_scatter, first=False):
            if has_next:
                for j in range(TPS):
                    power(st[:, 2 + j:3 + j], st[:, 4 + j:5 + j], S["xms"], xt.step(), S["xrs"])
            if has_in:
                for j in range(CH):
                    amul(s, j, has_post)
                    if j < CH - 1:
                        diff(s, j, first, has_post)
            if has_post:
                for j in range(TPS):
                    power(st[:, 6:7], st[:, 7:8], S["lnv"], lt_i.now + j + 1, S["lnr"])
            if has_in:
                diff(s, CH - 1, first, has_post)
            z.step((CH if has_post else 0) + (ZC if has_in else 0) + (TPS if has_post else 0))
            if has_scatter:
                scatter(s - 3)
            if has_post:
                for j in range(TPS):
                    power(st[:, 9:10], st[:, 10:11], S["x1_ms"], lt_i.step(), S["x1_rs"])

        for j in range(TPS):
            power(st[:, 2 + j:3 + j], st[:, 4 + j:5 + j], S["xms"], xt.step(), S["xrs"])
        pool.wait_ge(S["const_in"], 128)
        pool.wait_ge(S["init_st"], 32)
        step(0, True, True, False, False, first=True)
        step(1, True, True, True, False)
        step(2, True, True, True, False)
        with rolled(pool, NSUP - 4, {z: CH + ZC + TPS, xt: TPS, lt_i: TPS}) as i:
            step(i + 3, True, True, True, True)
        step(NSUP - 1, True, False, True, True)
        power(st[:, 2:3], st[:, 4:5], S["xms"], xt.step(), S["xrs"], NS)
        step(NSUP, False, False, True, True)
        scatter(NSUP - 2)
        power(st[:, 6:7], st[:, 7:8], S["lnv"], lt_i.now + 1, S["lnr"], NS)
        power(st[:, 9:10], st[:, 10:11], S["x1_ms"], lt_i.step(), S["x1_rs"], NS)
        scatter(NSUP - 1)
        scatter(NSUP, 1, NS)
        pool.wait_ge(S["scat"][0], 16 * TOPK * (NSUP + 1))
        pool.wait_ge(S["scat"][1], 16 * TOPK * NSUP)

        def gather(b, j):
            G.indirect_dma_start(xg[j][:], None, hf_d, bass.IndirectOffsetOnAxis(ap=gidx[j][:, 0:1], axis=0)).then_inc(S["gath"][j], 16)

        pool.wait_ge(S["cnt_ready"], 2)
        front_stored(pool)
        for b in range(2):
            G.iota(gidx[b][:], [[0, 1]], base=b * P, channel_multiplier=1).then_inc(S["pool_const"], 1)
        pool.wait_ge(S["pool_const"], 11)
        for b in range(2):
            gather(b, b)

        pool.wait_ge(S["tables_ready"], 1)
        pool.wait_ge(S["table_in"], 16)
        nblk = pool.value_load(ctab[0:1, NE:NE + 1], min_val=EB, max_val=MAXB)

        def ids(b, dst_):
            col = pool.value_load(btab[0:1, 0, ds(b, 1)], min_val=0, max_val=PADCOL)
            G.tensor_copy(dst_[:], lt[:, ds(col, 1), 0]).then_inc(S["pool_link"], 1)
            linked.wait(S["pool_link"])

        pool.wait_ge(S["gx_filled"], 2)
        ids(2, gidx[0])
        gather(2, 0)

        def turn(q):
            for h in range(2):
                b = 2 * q + 1 + h
                j = (1 + h) % 2
                pool.wait_ge(S["gx_filled"], 2 * b + 2)
                ids(b + 2, gidx[j])
                gather(b + 2, j)
                ids(b - 1, sidx[1 - j])
                pool.wait_ge(S["o_act"], b)
                pool.wait_ge(S["o_dve"], b)
                if isinstance(q, int):
                    wait(pool, S["scatb"], 16 * (b - 1))
                else:
                    added.wait(S["scatb"])
                G.indirect_dma_start(acc_d, bass.IndirectOffsetOnAxis(ap=sidx[1 - j][:, 0:1], axis=0),
                                     ob[1 - j][:], None, compute_op=ALU.add).then_inc(S["scatb"], 16)

        turn(0)
        with pool.Fori(0, (MAXB - 1) // 2) as q:
            with pool.If(2 * q + 2 < nblk):
                turn(q + 1)
        pool.wait_ge(S["smod_in"], 16 * 10)

        def end(i, j, stores, B, nt=P):
            power(fst[:, FB + j:FB + j + 1], fst[:, 2 * FB + j:2 * FB + j + 1], S["f_ms"], i + 1, S["f_rs"], nt)
            pool.wait_ge(S["f_aff"], i + 1)
            wait(pool, S["fin_st"][j], 16 * stores)
            G.tensor_tensor(fy[j][0:nt, :], fa[j][0:nt, :], B[:], ALU.add).then_inc(S["f_y"], 1)

        for j in range(FB):
            end(j, j, 0, Bfb)
        with pool.Fori(0, NTILE // FB - 1) as q:
            for j in range(FB):
                end(FB * q + j + FB, j, q + 1, Bfb)
        end(NTILE, 0, NTILE // FB, Bfs, NS)

    @block.scalar
    def _(act):
        A = nc.scalar
        tpu, z, xt, ti, wn, zp = Tally(), Tally(), Tally(), Tally(), Tally(), Tally()
        act.wait_ge(S["c_in"], 32)
        A.activation(cs9[:], c9[:], ACT.Sigmoid).then_inc(S["csig"], 1)
        act.wait_ge(S["prep_pe"], 1)
        A.copy(cT[:].rearrange("p k c -> p (k c)"), ly[:, 0:KD * NC]).then_inc(S["prep_act"], 1)
        act.wait_ge(S["prep_pe"], 2)
        A.copy(vecT[:], ms[:, 0:24]).then_inc(S["prep_act"], 1)
        A.copy(wdw[:].rearrange("p c t -> p (c t)"), ms[:, 32:32 + CH * TAPS]).then_inc(S["prep_act"], 1)

        nx, n1 = Tally(), Tally()

        def square(src, dst_, done, nt=P):
            wait(act, S["xsq"], nx.now)
            wait(act, S["x1_sq"], n1.now)
            (nx if done is S["xsq"] else n1).step()
            A.activation(junk[0:nt, :], src[0:nt, :], ACT.Square, accum_out=dst_[0:nt]).then_inc(done, 1)

        def x_square(j, count):
            act.wait_ge(S["xin_in"][j], 16 * count)
            square(xin[j], st[:, j:j + 1], S["xsq"])

        def xt_drain(j):
            n = xt.now
            for h in range(2):
                act.wait_ge(S["xt_filled"], 2 * n + h + 1)
                for kk in range(4):
                    k = 4 * h + kk
                    last = A.activation(hT[:, k, j * P:(j + 1) * P], tp[h][:, kk * P:(kk + 1) * P], ACT.Identity,
                                        scale=A1T[:, k, NS:NC], bias=B1T[:, k, NS:NC])
                last.then_inc(S["tp_drained"], 1)
            xt.step(); tpu.step()

        def pool_drain(nt=SUP):
            for g_ in range(CH):
                act.wait_ge(S["zp_filled"], zp.step())
                A.activation(mixP[:, g_, 0:nt], zb[z.n % 2][:, 0:nt], ACT.Copy, scale=vecT[:, 12 + g_:13 + g_]).then_inc(S["z_drained"], 1)
                z.step()

        def win_drain(s, first, part):
            for g_ in range(CH if part == 0 else 0):
                act.wait_ge(S["zw_filled"], wn.step())
                if not first:
                    act.wait_ge(S["d_ready"], CH * (s - 1) + g_ + 1)
                A.copy(u_buf[:, g_, POOLB:POOLB + SUP], zb[z.n % 2][:, 0:SUP]).then_inc(S["z_drained"], 1)
                z.step()
            for j in ((0,) if part == 0 else (1, 2, 3)):
                act.wait_ge(S["zw_filled"], wn.step())
                if not (first and j < 2):
                    act.wait_ge(S["a_ready"], CH * s + j - 1)
                A.activation(sgt[:, j % 2, :], zb[z.n % 2][:, 0:SUP], ACT.Sigmoid).then_inc(S["z_drained"], 1)
                z.step()
                act.wait_ge(S["zw_filled"], wn.step())
                A.copy(vv[:, j % 2, :], zb[z.n % 2][:, 0:SUP]).then_inc(S["z_drained"], 1)
                z.step()

        def ln_drain(j, nt=P):
            act.wait_ge(S["zl_filled"], ti.now + j + 1)
            for c in range(CH):
                last = A.activation(mixC[:, j, c, 0:nt], zb[z.n % 2][:, c * P:c * P + nt], ACT.Silu,
                                    scale=vecT[:, 4 + c:5 + c], bias=vecT[:, 8 + c:9 + c])
            last.then_inc(S["z_drained"], 1)
            z.step()

        def x1_square(j, nt=P):
            act.wait_ge(S["x1_ready"], ti.now + j + 1)
            square(x1b, st[:, 8:9], S["x1_sq"], nt)

        def h_drain(i, nt=P):
            for h in range(2):
                act.wait_ge(S["h_filled"], 2 * i + h + 1)
                A.copy(h2T[:, 4 * h:4 * h + 4, 0:nt], tp[h][:].rearrange("p (k t) -> p k t", k=4)[:, :, 0:nt]).then_inc(S["tp_drained"], 1)
            tpu.step()

        def gate_sigmoid(i, j, routed, nt=P):
            act.wait_ge(S["lg_filled"], i + 1)
            if routed is not None:
                wait(act, S["m_ready"], routed)
            A.activation(sg_r[0:nt, j, :], ms[0:nt, 0:NE], ACT.Sigmoid).then_inc(S["lg_drained"], 1)

        def step(s, has_in, has_next, has_post, has_late, first=False):
            i = ti.now
            if has_next:
                for j in range(TPS):
                    x_square(j, s + 2)
            if has_post:
                pool_drain()
            if has_in:
                win_drain(s, first, 0)
            if has_late:
                h_drain(i - 1)
                gate_sigmoid(i - 1, 1, None)
            if has_in:
                win_drain(s, first, 1)
            if has_next:
                for j in range(TPS):
                    xt_drain(j)
            if has_post:
                for j in range(TPS):
                    ln_drain(j)
                x1_square(0)
                h_drain(i)
                gate_sigmoid(i, 0, s - 1)
                x1_square(1)
                ti.step(TPS)

        x_square(0, 1)
        x_square(1, 1)
        act.wait_ge(S["aff_ready"], 2)
        for j in range(TPS):
            xt_drain(j)
        step(0, True, True, False, False, first=True)
        step(1, True, True, True, False)
        with rolled(act, NSUP - 3, {tpu: 2 * TPS, z: CH + ZC + TPS, xt: TPS, ti: TPS, wn: ZC, zp: CH, nx: TPS, n1: TPS}) as i:
            step(i + 2, True, True, True, True)
        step(NSUP - 1, True, False, True, True)
        act.wait_ge(S["state_in"], 64)
        square(xs, st[:, 0:1], S["xsq"], NS)
        for h in range(2):
            act.wait_ge(S["xt_filled"], 2 * NTILE + h + 1)
            A.copy(xsT[:, 4 * h:4 * h + 4, :], tp[h][:].rearrange("p (k t) -> p k t", k=4)[:, :, 0:NS]).then_inc(S["tp_drained"], 1)
        act.wait_ge(S["zw_filled"], wn.step())
        zv = zb[z.n % 2][:, 0:ZC * NS].rearrange("p (c t) -> p c t", c=ZC)
        A.copy(usm[:], zv[:, 0:CH, :])
        A.copy(asm[:], zv[:, CH:2 * CH, :])
        A.activation(gsm[:], zv[:, 2 * CH:3 * CH, :], ACT.Sigmoid).then_inc(S["z_drained"], 1)
        z.step()
        for i in range(3):
            act.wait_ge(S["edge_tp"], i + 1)
            src = zb[z.n % 2][:].rearrange("p (c r) -> p c r", c=CH)
            if i == 0:
                v_, d_ = src[:, :, 0:NS * POOLB].rearrange("p c (b t) -> p c b t", b=NS), full_p[:, :, :, 0:POOLB]
            else:
                v_, d_ = src[:, :, 0:4 * CONVB].rearrange("p c (b t) -> p c b t", b=4), full_c[:, :, 4 * i - 4:4 * i, 0:CONVB]
            for c in range(CH):
                last = A.copy(d_[:, c], v_[:, c])
            last.then_inc(S["z_drained"], 1)
            z.step()
        step(NSUP, False, False, True, True)
        h_drain(NTILE - 1)
        gate_sigmoid(NTILE - 1, 1, None)
        pool_drain(NS)
        ln_drain(0, NS)
        x1_square(0, NS)
        for i, n in enumerate((POOLB, CONVB, NS, NS)):
            act.wait_ge(S["edge_tp"], 4 + i)
            A.copy(edge[0:n, i, :], zb[z.n % 2][0:n, :]).then_inc(S["edge_ready"], 1)
            z.step()
        h_drain(NTILE, NS)
        gate_sigmoid(NTILE, 0, NSUP, NS)
        act.wait_ge(S["tables_ready"], 1)
        nblk = act.value_load(ctab[0:1, NE:NE + 1], min_val=EB, max_val=MAXB)

        def silu(b, j):
            act.wait_ge(S["gu_filled"], b + 1)
            A.activation(sgx[j][:], zb[j][:, 0:DE], ACT.Silu).then_inc(S["sg_ready"], 1)

        def gx(b):
            for h in range(2):
                act.wait_ge(S["gx_filled"], 2 * b + h + 1)
                A.copy(xh[:, 4 * h:4 * h + 4, :], tp[h][:].rearrange("p (k t) -> p k t", k=4)).then_inc(S["gx_hi"], 1)

        def ht(b):
            act.wait_ge(S["ht_filled"], b + 1)
            A.copy(hth[:].rearrange("p k t -> p (k t)"), ly[:, 0:DE]).then_inc(S["ht_hi"], 1)

        def round_w(sn, units):
            for u in units:
                A.copy(wh[:, ds(sn * UW + u, 1), :], stage[:, ds(sn * UW + u, 1), :]).then_inc(S["w_hi"], 1)

        landed = Goal(act, "act_landed", 3 * 48, 48)
        front_stored(act)
        act.wait_ge(S["w_landed"], 48)
        round_w(0, range(UG))
        gx(0)
        round_w(0, range(UG, UW))
        silu(0, 0)
        gx(1)
        act.wait_ge(S["w_landed"], 96)
        round_w(1, range(UG))
        ht(0)

        def turn(q):
            for h in range(2):
                b, j = 2 * q + 1 + h, (1 + h) % 2
                silu(b, j)
                gx(b + 1)
                sn = act.value_load(btab[0:1, 2, ds(b, 1)], min_val=0, max_val=1)
                begins = act.value_load(btab[0:1, 3, ds(b, 1)], min_val=0, max_val=1)
                goes_on = act.value_load(btab[0:1, 4, ds(b, 1)], min_val=0, max_val=1)
                with act.If(begins > 0):
                    landed.wait(S["w_landed"])
                    round_w(sn, range(UG))
                act.wait_ge(S["o_filled"], b)
                wait(act, S["scatb"], 16 * (b - 2))
                A.copy(ob[1 - j][:, 0:512], mx[0][:]).then_inc(S["o_act"], 1)
                ht(b)
                with act.If(goes_on > 0):
                    round_w(sn, range(UG, UW))

        turn(0)
        with act.Fori(0, (MAXB - 1) // 2) as q:
            with act.If(2 * q + 2 < nblk):
                turn(q + 1)

        def fsq(i, j, nt=P):
            act.wait_ge(S["f_sum"], i + 1)
            A.activation(fjunk[0:nt, :], fa[j][0:nt, :], ACT.Square, accum_out=fst[0:nt, j:j + 1]).then_inc(S["f_sq"], 1)

        with act.Fori(0, NTILE // FB) as q:
            for j in range(FB):
                fsq(FB * q + j, j)
        fsq(NTILE, 0, NS)

    @block.vector
    def _(dve):
        V = nc.vector
        cv, xt, ti = Tally(), Tally(), Tally()
        linked = Goal(dve, "dve_linked", 1, 1)

        def chain(ins):
            ins.then_inc(S["dve_link"], 1)
            linked.wait(S["dve_link"])

        V.memset(a_buf[:], 0.0).then_inc(S["dve_const"], 1)
        V.memset(Macc[:], 0.0).then_inc(S["dve_const"], 1)
        dve.wait_ge(S["dve_const"], 2)
        dve.wait_ge(S["csig"], 1)
        dve.wait_ge(S["c_in"], 32)
        V.tensor_tensor(c9[:], c9[:], cs9[:], ALU.mult).then_inc(S["c_ready"], 1)

        def mod_drain(n):
            dve.wait_ge(S["mod_filled"], n + 1)
            dve.wait_ge(S["adab_in"][n % 2], 16 * (n // 2 + 1))
            if n >= 4:
                dve.wait_ge(S["modrow_st"][n % 4], 16 * (n // 4))
                if n < 8:
                    dve.wait_ge(S["mod1_t"], 1)
            V.tensor_tensor(mrow[:, n % 4, :], zb[n % 2][0:NC, :], mbias[:, n % 2, :], ALU.add).then_inc(S["mod_drained"], 1)

        for n in range(4):
            mod_drain(n)
        dve.wait_ge(S["mod1_t"], 1)
        dve.wait_ge(S["prep_act"], 2)
        V.tensor_copy(B1T[:].rearrange("p k c -> p (k c)"), tp[0][:, 0:KD * NC]).then_inc(S["aff_ready"], 1)
        for k in range(KD):
            last = V.tensor_scalar(A1T[:, k, :], tp[0][:, (KD + k) * NC:(KD + k + 1) * NC], 1.0, vecT[:, 16 + k:17 + k], ALU.add, ALU.mult)
        last.then_inc(S["aff_ready"], 1)

        def xn_ms(j, nt=P):
            dve.wait_ge(S["xsq"], xt.now + 1)
            V.tensor_scalar(st[0:nt, 2 + j:3 + j], st[0:nt, j:j + 1], 1.0 / D, EPS, ALU.mult, ALU.add).then_inc(S["xms"], 1)
            xt.step()

        def xn(j, n, nt=P):
            dve.wait_ge(S["xrs"], n)
            V.tensor_scalar(xin[j][0:nt, :], xin[j][0:nt, :], st[0:nt, 4 + j:5 + j], None, ALU.mult).then_inc(S["xn_ready"], 1)

        def conv(p, first):
            dve.wait_ge(S["a_ready"], CH * p + CH)
            if not first:
                chain(V.tensor_copy(a_buf[:, :, 0:CONVB], a_buf[:, :, SUP:SUP + CONVB]))
            V.tensor_copy(a_buf[:, :, CONVB:CONVB + SUP], av[:]).then_inc(S["a_taken"], 1)
            dve.wait_ge(S["a_taken"], p + 1)
            if not first:
                dve.wait_ge(S["ly_filled"], ti.now)
            for k in range(TAPS):
                for c in range(CH):
                    win_ = a_buf[:, c, k:k + SUP]
                    if k == 0:
                        ins = V.tensor_scalar(y[:, c, :], win_, wdw[:, c, 0:1], vecT[:, c:c + 1], ALU.mult, ALU.add)
                    else:
                        dve.wait_ge(S["conv_link"], cv.now - CH + 1)
                        ins = V.scalar_tensor_tensor(y[:, c, :], win_, wdw[:, c, k:k + 1], y[:, c, :], ALU.mult, ALU.add)
                    ins.then_inc(S["conv_link"], 1)
                    cv.step()

        def norm(i, nt=P):
            dve.wait_ge(S["ly_filled"], i + 1)
            chain(V.bn_stats(bn6[0:nt, :], ly[0:nt, :]))
            chain(V.bn_aggr(bn2[0:nt, :], bn6[0:nt, :]))
            V.tensor_scalar(st[0:nt, 6:7], bn2[0:nt, 1:2], EPS, None, ALU.add).then_inc(S["lnv"], 1)
            dve.wait_ge(S["lnr"], i + 1)
            V.tensor_scalar(yn[0:nt, :], ly[0:nt, :], bn2[0:nt, 0:1], st[0:nt, 7:8], ALU.subtract, ALU.mult).then_inc(S["ly_drained"], 1)

        def residual(i, first, nt=P):
            dve.wait_ge(S["mix_filled"], i + 1)
            dve.wait_ge(S["xres_in"], 16 * i + 16)
            if not first:
                dve.wait_ge(S["x1_st"], 16 * i)
            for n in range(2):
                last = V.tensor_tensor(x1b[0:nt, n * 512:(n + 1) * 512], mx[n][0:nt, :], g1b[0:nt, n * 512:(n + 1) * 512], ALU.mult)
            last.then_inc(S["mix_drained"], 1)
            dve.wait_ge(S["mix_drained"], i + 1)
            V.tensor_tensor(x1b[0:nt, :], x1b[0:nt, :], xres[0:nt, :], ALU.add).then_inc(S["x1_ready"], 1)

        def mixer_in(i, first, nt=P):
            dve.wait_ge(S["x1_sq"], i + 1)
            V.tensor_scalar(st[0:nt, 9:10], st[0:nt, 8:9], 1.0 / D, EPS, ALU.mult, ALU.add).then_inc(S["x1_ms"], 1)
            dve.wait_ge(S["x1_rs"], i + 1)
            if not first:
                dve.wait_ge(S["h2_st"], 16 * i)
                dve.wait_ge(S["h_filled"], 2 * i)
            chain(V.scalar_tensor_tensor(h2[0:nt, :], x1b[0:nt, :], st[0:nt, 10:11], A2b[0:nt, :], ALU.mult, ALU.mult))
            V.tensor_tensor(h2[0:nt, :], h2[0:nt, :], B2b[0:nt, :], ALU.add).then_inc(S["h2_ready"], 1)

        def route(lg, tiles=TPS, nt=P):
            dve.wait_ge(S["lg_drained"], lg)
            n, w, wg = slice(0, nt), slice(0, tiles), slice(0, tiles * NG)
            chain(V.tensor_tensor(sel[n, w], sg_r[n, w], router_b[n].unsqueeze(1).to_broadcast([nt, tiles, NE]), ALU.add))
            sel8 = sel[:].rearrange("p t (g e) -> p (t g) e", g=NG)[n, wg]
            for q in range(tiles * NG):
                last = V.max(m8[n, q, :], sel8[:, q, :])
            chain(last)
            gsc_ = gsc[:].rearrange("p t g -> p (t g)")[n, wg]
            chain(V.tensor_tensor(gsc_, m8[n, wg, 0], m8[n, wg, 1], ALU.add))
            for t in range(tiles):
                last = V.max(gm[n, t, :], gsc[n, t, :])
            chain(last)
            for t in range(tiles):
                last = V.max_index(gi[n, t, :], gm[n, t, :], gsc[n, t, :])
            chain(last)
            chain(V.tensor_copy(gif[n, w], gi[n, w]))
            for t in range(tiles):
                last = V.tensor_tensor(oh4[n, t], iota64[n, 0:NG].unsqueeze(2).to_broadcast([nt, NG, TOPG]),
                                       gif[n, t, 0:TOPG].unsqueeze(1).to_broadcast([nt, NG, TOPG]), ALU.is_equal)
            chain(last)
            chain(V.tensor_reduce(gmask[n, wg], oh4[:].rearrange("p t g k -> p (t g) k")[n, wg], AX.X, ALU.add))
            chain(V.tensor_scalar(pen[n, wg], gmask[n, wg], 1.0, BIG, ALU.subtract, ALU.mult))
            chain(V.tensor_tensor(sel8, sel8, gmask[n, wg].unsqueeze(2).to_broadcast([nt, tiles * NG, 8]), ALU.mult))
            chain(V.tensor_tensor(sel8, sel8, pen[n, wg].unsqueeze(2).to_broadcast([nt, tiles * NG, 8]), ALU.add))
            for t in range(tiles):
                last = V.max(gm[n, t, :], sel[n, t, :])
            chain(last)
            for t in range(tiles):
                last = V.max_index(gi[n, t, :], gm[n, t, :], sel[n, t, :])
            chain(last)
            chain(V.tensor_copy(gif[n, w], gi[n, w]))
            for t in range(tiles):
                last = V.tensor_tensor(oh[n, t], iota64[n, :].unsqueeze(1).to_broadcast([nt, TOPK, NE]),
                                       gif[n, t, :].unsqueeze(2).to_broadcast([nt, TOPK, NE]), ALU.is_equal)
            chain(last)
            for t in range(tiles):
                last = V.tensor_tensor(prod[n, t], oh[n, t], sg_r[n, t, :].unsqueeze(1).to_broadcast([nt, TOPK, NE]), ALU.mult)
            chain(last)
            V.tensor_reduce(Mt[n, w], oh[n, w].rearrange("p t k e -> p t e k"), AX.X, ALU.add).then_inc(S["m_ready"], 1)
            chain(V.tensor_reduce(wk[n, w], prod[n, w], AX.X, ALU.add))
            chain(V.tensor_reduce(wsum[n, 0, w], wk[n, w], AX.X, ALU.add))
            chain(V.reciprocal(wsum[n, 1, w], wsum[n, 0, w]))

        def slots(group, tiles=TPS, nt=P):
            n, w = slice(0, nt), slice(0, tiles)
            dve.wait_ge(S["rk_filled"], group + 1)
            V.tensor_copy(ri[n, 0, w], ms[:, NE:3 * NE].rearrange("p (t e) -> p t e", t=TPS)[n, w]).then_inc(S["rk_drained"], 1)
            for t in range(tiles):
                chain(V.tensor_tensor(Macc[n, :], Macc[n, :], Mt[n, t], ALU.add))
            dve.wait_ge(S["rk_drained"], group + 1)
            V.tensor_single_scalar(ri[n, 1, w], ri[n, 0, w], P - 1, ALU.bitwise_and)
            chain(V.tensor_single_scalar(ri[n, 2, w], ri[n, 0, w], 7, ALU.arith_shift_right))
            chain(V.tensor_scalar(dst[n, w], ri[n, 1, w], float(NCOL), None, ALU.mult))
            chain(V.tensor_tensor(dst[n, w], dst[n, w], ri[n, 2, w], ALU.add))
            chain(V.tensor_tensor(dst[n, w], dst[n, w], base17[n, :].unsqueeze(1).to_broadcast([nt, tiles, NE]), ALU.add))
            for t in range(tiles):
                last = V.tensor_tensor(prod[n, t], oh[n, t], dst[n, t, :].unsqueeze(1).to_broadcast([nt, TOPK, NE]), ALU.mult)
            chain(last)
            chain(V.tensor_reduce(dk[n, w], prod[n, w], AX.X, ALU.add))
            lists_free(group)
            chain(V.tensor_scalar(tokid[:], tokid[:], float(SUP), None, ALU.add))
            for t in range(tiles):
                V.tensor_copy(pairs[n, t, :, 0], tokid[n, t:t + 1].to_broadcast([nt, TOPK]))
                last = V.tensor_scalar(pairs[n, t, :, 1].bitcast(F32), wk[n, t, :], wsum[n, 1, t:t + 1], SCALE, ALU.mult, ALU.mult)
            chain(last)
            V.tensor_copy(rows[n, w], dk[n, w]).then_inc(S["pairs_ready"], 1)

        def lists_free(group):
            for q in S["scat"]:
                wait(dve, q, 16 * TOPK * group)

        def step(s, has_next, has_post, has_late, kind=""):
            if has_next:
                for j in range(TPS):
                    xn_ms(j)
                for j in range(TPS):
                    xn(j, xt.now - 1 + j)
            if has_post:
                conv(s - 1, kind == "second")
            if has_post:
                if kind == "second":
                    bcast(h2)
                    dve.wait_ge(S["zero_st"], 32)
                for j in range(TPS):
                    norm(ti.now + j)
                if has_late:
                    route(ti.now)
                for j in range(TPS):
                    residual(ti.now + j, kind == "second" and j == 0)
                    mixer_in(ti.now + j, kind == "second" and j == 0)
                    if has_late and j == 0:
                        slots(s - 2)
                ti.step(TPS)

        def bcast(gain, nt=P, sem_=None):
            dve.wait_ge(S["bc_in"], 64)
            chain(V.scalar_tensor_tensor(A2b[0:nt, :], A2b[0:nt, :], 1.0, gain[0:nt, :], ALU.add, ALU.mult))

        for j in range(TPS):
            xn_ms(j)
        for j in range(TPS):
            xn(j, j + 1)
        for n in range(4, SBLK):
            mod_drain(n)
        dve.wait_ge(S["const_in"], 128)
        dve.wait_ge(S["small_in"], 144)
        dve.wait_ge(S["prep_act"], 3)
        dve.wait_ge(S["pool_const"], 9)
        step(0, True, False, False)
        step(1, True, True, False, kind="second")
        step(2, True, True, True)
        with rolled(dve, NSUP - 4, {cv: CH * TAPS, xt: TPS, ti: TPS}) as i:
            step(i + 3, True, True, True)
        step(NSUP - 1, False, True, True)
        xn_ms(0, NS)
        dve.wait_ge(S["xrs"], NTILE + 1)
        V.tensor_scalar(xs[:], xs[:], st[0:NS, 4:5], None, ALU.mult).then_inc(S["xn_ready"], 1)
        dve.wait_ge(S["tp_drained"], 2 * (2 * NTILE - TPS))
        chain(V.tensor_tensor(xsT[:], xsT[:], A1T[:, :, 0:NS], ALU.mult))
        V.tensor_tensor(hT[:, :, 0:NS], xsT[:], B1T[:, :, 0:NS], ALU.add).then_inc(S["sm_h"], 1)
        step(NSUP, False, True, True)
        zs = (NSUP - 1) * (CH + TPS) + NSUP * ZC
        dve.wait_ge(S["z_drained"], zs + 1)
        chain(V.tensor_tensor(asm[:], asm[:], gsm[:], ALU.mult))
        dve.wait_ge(S["z_drained"], zs + 4)
        chain(V.tensor_copy(full_c[:, :, :, CONVB], asm[:]))
        chain(V.tensor_copy(full_p[:, :, :, POOLB], usm[:]))
        for c in range(CH):
            w = 2 << c
            pc = prod[:].rearrange("p t k e -> p (t k e)")[:, 0:NS * TAPS].rearrange("p (b t) -> p b t", b=NS)
            chain(V.tensor_tensor(pc, full_c[:, c], wdw[:, c, :].unsqueeze(1).to_broadcast([P, NS, TAPS]), ALU.mult))
            chain(V.tensor_reduce(ysm[:, c, :], pc, AX.X, ALU.add))
            chain(V.tensor_scalar(ysm[:, c, :], ysm[:, c, :], vecT[:, c:c + 1], None, ALU.add))
            chain(V.tensor_reduce(dsm[:, c, :], full_p[:, c, :, 16 - w:16], AX.X, ALU.add))
            last = V.scalar_tensor_tensor(dsm[:, c, :], dsm[:, c, :], 1.0 / w, usm[:, c, :], ALU.mult, ALU.subtract)
            if c < CH - 1:
                chain(last)
        last.then_inc(S["sm_y"], 1)
        dve.wait_ge(S["smod_in"], 48)
        dve.wait_ge(S["xin_in"][1], 16 * (NSUP + 1))
        chain(V.scalar_tensor_tensor(A2b[0:NS, :], A2b[0:NS, :], 1.0, xin[1][0:NS, :], ALU.add, ALU.mult))
        norm(NTILE, NS)
        route(NTILE)
        residual(NTILE, False, NS)
        mixer_in(NTILE, False, NS)
        slots(NSUP - 1)
        route(NTILE + 1, 1, NS)
        slots(NSUP, 1, NS)
        dve.wait_ge(S["cnt_filled"], 1)
        chain(V.tensor_copy(cnt[:], ms[0:NE, 0:1]))
        chain(V.tensor_scalar(nbt[:], thr[:], cnt[:, 0:1], None, ALU.is_lt))
        V.tensor_reduce(nb[:], nbt[:], AX.X, ALU.add).then_inc(S["cnt_ready"], 1)
        dve.wait_ge(S["cnt_filled"], 2)
        chain(V.tensor_scalar(ccum[:], ms[0:NE, 0:1], float(EB), None, ALU.add))
        V.memset(ctab[0:1, 0:1], EB)
        chain(V.tensor_scalar(ctab[0:1, 1:NORD], ms[0:1, NE:2 * NE], float(EB), None, ALU.add))
        dve.wait_ge(S["row_in"], 32)
        V.tensor_scalar(amat[:], biota[:], ccum[:, 0:1], None, ALU.is_ge).then_inc(S["cnt_ready"], 1)
        dve.wait_ge(S["cnt_filled"], 3)
        e_, s_, cb, mk = tabf[0:1, 0, :], tabf[0:1, 1, :], brow[0:1, 0, :], brow[0:1, 1, :]
        t2, t3, t4 = tabf[0:1, 2, :], tabf[0:1, 3, :], tabf[0:1, 4, :]
        V.tensor_copy(e_, ms[0:1, 0:NBT])
        chain(V.tensor_copy(s_, zb[0][0:1, 0:NBT]))
        chain(V.tensor_scalar(t2, e_, float(EB), None, ALU.mult))
        chain(V.tensor_tensor(t2, t2, cb, ALU.add))
        chain(V.tensor_tensor(t2, t2, s_, ALU.subtract))
        chain(V.tensor_scalar(t3, e_, float(NE), None, ALU.is_ge))
        chain(V.tensor_scalar(t4, t2, -1.0, float(PADCOL), ALU.mult, ALU.add))
        chain(V.tensor_tensor(t4, t4, t3, ALU.mult))
        chain(V.tensor_tensor(t2, t2, t4, ALU.add))
        V.tensor_copy(btab[0:1, 0, :], t2)
        chain(V.tensor_scalar(t3, e_, 1.0, float(NE), ALU.add, ALU.min))
        chain(V.tensor_tensor(t3, t3, mk, ALU.mult))
        t5, t6 = tabf[0:1, 5, :], tabf[0:1, 6, :]
        V.tensor_copy(btab[0:1, 1, :], t3)
        V.tensor_scalar(t2, t3, float(NE), None, ALU.is_lt)
        V.memset(t4, 0.0)
        chain(V.memset(t5, 1.0))
        V.tensor_single_scalar(btab[0:1, 2, :], btab[0:1, 1, :], 1, ALU.bitwise_and)
        chain(V.tensor_tensor(t5[:, 1:NBT], t3[:, 1:NBT], t3[:, 0:NBT - 1], ALU.subtract))
        chain(V.tensor_scalar(t6, t5, -1.0, 1.0, ALU.mult, ALU.add))
        chain(V.tensor_tensor(t4[:, 1:NBT - 1], t6[:, 1:NBT - 1], t5[:, 0:NBT - 2], ALU.mult))
        chain(V.tensor_tensor(t6[:, 1:NBT - 1], t5[:, 1:NBT - 1], t5[:, 2:NBT], ALU.mult))
        chain(V.tensor_tensor(t4[:, 1:NBT - 1], t4[:, 1:NBT - 1], t6[:, 1:NBT - 1], ALU.add))
        V.tensor_tensor(btab[0:1, 3, :], t5, t2, ALU.mult)
        V.tensor_tensor(btab[0:1, 4, :], t4, t2, ALU.mult)
        next_buffer = btab[0:1, 2, :]
        V.tensor_scalar(next_buffer, next_buffer, -1.0, 1.0, ALU.mult, ALU.add).then_inc(S["tables_ready"], 1)
        dve.wait_ge(S["tables_ready"], 1)
        nblk = dve.value_load(ctab[0:1, NE:NE + 1], min_val=EB, max_val=MAXB)

        def hidden(b, j):
            col = dve.value_load(btab[0:1, 0, ds(b, 1)], min_val=0, max_val=PADCOL)
            dve.wait_ge(S["sg_ready"], b + 1)
            V.scalar_tensor_tensor(hh[:], sgx[j][:], ltf[:, ds(2 * col + 1, 1)], zb[j][:, DE:2 * DE], ALU.mult, ALU.mult).then_inc(S["hh_ready"], 1)

        def gx(b):
            for h in range(2):
                k = slice(4 * h, 4 * h + 4)
                dve.wait_ge(S["gx_hi"], 2 * b + h + 1)
                V.tensor_tensor(xl[:, k, :], tp[h][:].rearrange("p (k t) -> p k t", k=4), xh[:, k, :].bitcast(F32), ALU.subtract).then_inc(S["gx_lo"], 1)

        def ht(b):
            dve.wait_ge(S["ht_hi"], b + 1)
            V.tensor_tensor(htl[:].rearrange("p k t -> p (k t)"), ly[:, 0:DE], hth[:].rearrange("p k t -> p (k t)").bitcast(F32), ALU.subtract).then_inc(S["ht_lo"], 1)

        rounded = Goal(dve, "dve_rounded", UW + UG + 1, 1)

        def rest_w(sn, units):
            for u in units:
                if isinstance(sn, int):
                    dve.wait_ge(S["w_hi"], UW * sn + u + 1)
                else:
                    rounded.wait(S["w_hi"])
                at = ds(sn * UW + u, 1)
                V.tensor_tensor(wl[:, at, :], stage[:, at, :], wh[:, at, :].bitcast(F32), ALU.subtract).then_inc(S["w_lo"], 1)

        front_stored(dve)
        rest_w(0, range(UG))
        gx(0)
        rest_w(0, range(UG, UW))
        dve.wait_ge(S["table_in"], 16)
        hidden(0, 0)
        gx(1)
        rest_w(1, range(UG))
        ht(0)

        def turn(q):
            for h in range(2):
                b, j = 2 * q + 1 + h, (1 + h) % 2
                dve.wait_ge(S["ht_filled"], b)
                hidden(b, j)
                gx(b + 1)
                sn = dve.value_load(btab[0:1, 2, ds(b, 1)], min_val=0, max_val=1)
                begins = dve.value_load(btab[0:1, 3, ds(b, 1)], min_val=0, max_val=1)
                goes_on = dve.value_load(btab[0:1, 4, ds(b, 1)], min_val=0, max_val=1)
                with dve.If(begins > 0):
                    rest_w(sn, range(UG))
                dve.wait_ge(S["o_filled"], b)
                wait(dve, S["scatb"], 16 * (b - 2))
                V.tensor_copy(ob[1 - j][:, 512:1024], mx[1][:]).then_inc(S["o_dve"], 1)
                ht(b)
                with dve.If(goes_on > 0):
                    rest_w(sn, range(UG, UW))

        turn(0)
        with dve.Fori(0, (MAXB - 1) // 2) as q:
            with dve.If(2 * q + 2 < nblk):
                turn(q + 1)

        dve.wait_ge(S["smod_in"], 16 * 10)
        V.scalar_tensor_tensor(Afs[:], Afs[:], 1.0, gfb[0:NS, :], ALU.add, ALU.mult)
        chain(V.scalar_tensor_tensor(Afb[:], Afb[:], 1.0, gfb[:], ALU.add, ALU.mult))

        def gated(i, j, loads, g2_, nt=P):
            dve.wait_ge(S["fin_in"][j], 32 * loads)
            V.tensor_tensor(fa[j][0:nt, :], fa[j][0:nt, :], g2_[:], ALU.mult).then_inc(S["f_gated"], 1)

        def summed(i, j, nt=P):
            dve.wait_ge(S["f_gated"], i + 1)
            V.tensor_tensor(fa[j][0:nt, :], fa[j][0:nt, :], fx[j][0:nt, :], ALU.add).then_inc(S["f_sum"], 1)

        def mean(i, j, nt=P):
            dve.wait_ge(S["f_sq"], i + 1)
            V.tensor_scalar(fst[0:nt, FB + j:FB + j + 1], fst[0:nt, j:j + 1], 1.0 / D, EPS, ALU.mult, ALU.add).then_inc(S["f_ms"], 1)

        def scaled(i, j, A_, nt=P):
            dve.wait_ge(S["f_rs"], i + 1)
            V.scalar_tensor_tensor(fa[j][0:nt, :], fa[j][0:nt, :], fst[0:nt, 2 * FB + j:2 * FB + j + 1], A_[:], ALU.mult, ALU.mult).then_inc(S["f_aff"], 1)

        def both(i, j, loads, g2_=g2b, nt=P):
            gated(i + 1, (j + 1) % FB, loads, g2_, nt)
            mean(i, j)
            summed(i + 1, (j + 1) % FB, nt)
            scaled(i, j, Afb)

        gated(0, 0, 1, g2b)
        summed(0, 0)
        with dve.Fori(0, NTILE // FB - 1) as q:
            for j in range(FB):
                both(FB * q + j, j, q + 1 + (j == FB - 1))
        for j in range(FB - 1):
            both(NTILE - FB + j, j, NTILE // FB)
        both(NTILE - 1, FB - 1, NTILE // FB + 1, g2s, NS)
        mean(NTILE, 0, NS)
        scaled(NTILE, 0, Afs, NS)

    @block.tensor
    def _(pe):
        M = nc.tensor
        tpu, z, xt, ti, kd = Tally(), Tally(), Tally(), Tally(), Tally()
        pe.wait_ge(S["const_in"], 128)
        pe.wait_ge(S["c_ready"], 1)
        for k in range(KD):
            last = M.transpose(ly[:, k * NC:(k + 1) * NC], c9[:, k * P:(k + 1) * P], ident[0:NC, 0:NC])
        last.then_inc(S["prep_pe"], 1)
        pe.wait_ge(S["small_in"], 144)
        M.transpose(ms[:, 0:24], vecs[:], ident[0:24, 0:24])
        for c in range(CH):
            last = M.transpose(ms[:, 32 + c * TAPS:32 + (c + 1) * TAPS], dwr[0:TAPS, c * P:(c + 1) * P], ident[0:TAPS, 0:TAPS])
        last.then_inc(S["prep_pe"], 1)

        def mod(n):
            pe.wait_ge(S["ada_in"][n % 2], 16 * (n // 2 + 1))
            if n >= 2:
                pe.wait_ge(S["mod_drained"], n - 1)
            for k in range(KD):
                last = M.matmul(zb[n % 2][0:NC, :], cT[:, k, :], big[:, n % 2, k, :], start=(k == 0), stop=(k == KD - 1))
            last.then_inc(S["mod_filled"], 1)

        def rows_T(src, nt, done):
            u = tpu.now
            for h in range(2):
                wait(pe, S["tp_drained"], 2 * u + h - 1)
                for kk in range(4):
                    k = 4 * h + kk
                    last = M.transpose(tp[h][:, kk * P:kk * P + nt], src[0:nt, k * P:(k + 1) * P], ident[0:nt, 0:nt])
                last.then_inc(done, 1)
            tpu.step()

        def xT_(src, nt=P):
            pe.wait_ge(S["xn_ready"], xt.step())
            rows_T(src, nt, S["xt_filled"])

        def zbank():
            wait(pe, S["z_drained"], z.now - 1)
            b = zb[z.n % 2]
            z.step()
            return b

        def pool_mm(p, src, nt):
            for g_ in range(CH):
                b = zbank()
                M.matmul(b[:, 0:nt], w_pool[:, g_, :], src[:, g_, 0:nt], start=True, stop=True).then_inc(S["zp_filled"], 1)

        def w_in_mm(part):
            order = list(range(CH)) + [c for j in range(CH) for c in (2 * CH + j, CH + j)]
            for m in order[:CH + 2] if part == 0 else order[CH + 2:]:
                b = zbank()
                for k in range(KD):
                    last = M.matmul(b[:, 0:SUP], win[:, k, m * P:(m + 1) * P], hT[:, k, :], start=(k == 0), stop=(k == KD - 1))
                last.then_inc(S["zw_filled"], 1)

        def y_T(i, src, c0, nt=P):
            wait(pe, S["ly_drained"], i)
            for c in range(CH):
                last = M.transpose(ly[0:nt, c * P:(c + 1) * P], src[:, c, c0:c0 + nt], ident[:])
            last.then_inc(S["ly_filled"], 1)

        def yn_T(i, nt=P):
            pe.wait_ge(S["ly_drained"], i + 1)
            b = zbank()
            for c in range(CH):
                last = M.transpose(b[:, c * P:c * P + nt], yn[0:nt, c * P:(c + 1) * P], ident[0:nt, 0:nt])
            last.then_inc(S["zl_filled"], 1)

        def w_out_mm(i, j, zn, nt=P):
            pe.wait_ge(S["z_drained"], zn)
            wait(pe, S["mix_drained"], i)
            for n in range(2):
                for k in range(KD):
                    lhs = mixP[:, k, j * P:j * P + nt] if k < CH else mixC[:, j, k - CH, 0:nt]
                    last = M.matmul(mx[n][0:nt, :], lhs, big[:, n, k, :], start=(k == 0), stop=(k == KD - 1))
            last.then_inc(S["mix_filled"], 1)

        def h_T(i, nt=P):
            pe.wait_ge(S["h2_ready"], i + 1)
            rows_T(h2, nt, S["h_filled"])

        def logits(i, nt=P):
            pe.wait_ge(S["tp_drained"], 2 * tpu.now)
            wait(pe, S["lg_drained"], i)
            wait(pe, S["rk_drained"], kd.now)
            for k in range(KD):
                last = M.matmul(ms[0:nt, 0:NE], h2T[:, k, 0:nt], w_router[:, k, :], start=(k == 0), stop=(k == KD - 1))
            last.then_inc(S["lg_filled"], 1)

        def ranks(lg, tiles=TPS, nt=P):
            pe.wait_ge(S["lg_drained"], lg)
            wait(pe, S["rk_drained"], kd.now)
            pe.wait_ge(S["m_ready"], kd.now + 1)
            wait(pe, S["pairs_ready"], kd.now)
            for t in range(tiles):
                o = ms[0:nt, (1 + t) * NE:(2 + t) * NE]
                M.matmul(o, ones[:, 0:nt], Macc[:], start=True, stop=False)
                for before in range(t):
                    M.matmul(o, ones[0:nt, 0:nt], Mt[0:nt, before], start=False, stop=False)
                last = M.matmul(o, tri[0:nt, 0:nt], Mt[0:nt, t], start=False, stop=True)
            last.then_inc(S["rk_filled"], 1)
            kd.step()

        def step(s, has_in, has_next, has_post, has_late):
            i = ti.now
            if has_post:
                pe.wait_ge(S["d_ready"], CH * s)
                pool_mm(s - 1, dd, SUP)
            if has_in:
                pe.wait_ge(S["tp_drained"], 2 * tpu.now)
                w_in_mm(0)
            if has_late:
                h_T(i - 1)
                logits(i - 1)
            if has_in:
                w_in_mm(1)
            if has_next:
                xT_(xin[0])
            if has_post:
                pe.wait_ge(S["conv_link"], CH * TAPS * s)
                y_T(i, y, 0)
            if has_next:
                xT_(xin[1])
            if has_post:
                yn_T(i)
                z0 = z.now
                y_T(i + 1, y, P)
                w_out_mm(i, 0, z0)
                yn_T(i + 1)
                if has_late:
                    ranks(i)
                w_out_mm(i + 1, 1, z.now)
                h_T(i)
                logits(i)
                ti.step(TPS)

        pe.wait_ge(S["prep_act"], 3)
        for n in range(4):
            mod(n)
        pe.wait_ge(S["mod_drained"], 4)
        for m in range(2):
            for k in range(KD):
                src = mrow[:, 2 * m + k // 4, (k % 4) * P:(k % 4 + 1) * P]
                last = M.transpose(tp[0][:, (m * KD + k) * NC:(m * KD + k + 1) * NC], src, ident[0:NC, 0:NC])
        last.then_inc(S["mod1_t"], 1)
        pe.wait_ge(S["aff_ready"], 2)
        for j in range(TPS):
            xT_(xin[j])
        for n in range(4, SBLK):
            mod(n)
        pe.wait_ge(S["mod_drained"], SBLK)
        pe.wait_ge(S["win_in"], 16 * KD)
        step(0, True, True, False, False)
        pe.wait_ge(S["wout_in"], 32)
        step(1, True, True, True, False)
        step(2, True, True, True, True)
        with rolled(pe, NSUP - 4, {tpu: 2 * TPS, z: CH + ZC + TPS, xt: TPS, ti: TPS, kd: 1}) as i:
            step(i + 3, True, True, True, True)
        step(NSUP - 1, True, False, True, True)
        xT_(xs, NS)
        pe.wait_ge(S["sm_h"], 1)
        b = zbank()
        for m in range(ZC):
            for k in range(KD):
                last = M.matmul(b[:, m * NS:(m + 1) * NS], win[:, k, m * P:(m + 1) * P], hT[:, k, 0:NS], start=(k == 0), stop=(k == KD - 1))
        last.then_inc(S["zw_filled"], 1)
        pe.wait_ge(S["state_in"], 64)
        for i, nr in enumerate((NS * POOLB, 4 * CONVB, 4 * CONVB)):
            b = zbank()
            for c in range(CH):
                last = M.transpose(b[:, c * P:c * P + nr], strow[i][0:nr, c * P:(c + 1) * P], ident[0:nr, 0:nr])
            last.then_inc(S["edge_tp"], 1)
        step(NSUP, False, False, True, True)
        h_T(NTILE - 1)
        logits(NTILE - 1)
        pe.wait_ge(S["sm_y"], 1)
        pool_mm(NSUP, dsm, NS)
        y_T(NTILE, ysm, 0, NS)
        yn_T(NTILE, NS)
        w_out_mm(NTILE, 0, z.now, NS)
        edges = [(u_buf, 0, POOLB), (a_buf, SUP, CONVB), (usm, 0, NS), (asm, 0, NS)]
        for i, (t, c0, n) in enumerate(edges):
            if i < 2:
                wait(pe, S["z_drained"], z.now - 1)
            else:
                pe.wait_ge(S["edge_ready"], i - 1)
            b = zb[z.n % 2]
            z.step()
            for c in range(CH):
                last = M.transpose(b[0:n, c * P:(c + 1) * P], t[:, c, c0:c0 + n], ident[:])
            last.then_inc(S["edge_tp"], 1)
        pe.wait_ge(S["edge_ready"], 4)
        ranks(NTILE)
        h_T(NTILE, NS)
        logits(NTILE, NS)
        ranks(NTILE + 1, 1, NS)
        pe.wait_ge(S["pairs_ready"], NSUP + 1)
        M.matmul(ms[0:NE, 0:1], Macc[:], ones[:, 0:1], start=True, stop=True).then_inc(S["cnt_filled"], 1)
        pe.wait_ge(S["cnt_ready"], 1)
        M.matmul(ms[0:NE, 0:1], uinc[:], nb[:], start=True, stop=True)
        M.matmul(ms[0:1, NE:2 * NE], nb[:], uinc[:], start=True, stop=True).then_inc(S["cnt_filled"], 1)
        pe.wait_ge(S["cnt_ready"], 2)
        M.matmul(ms[0:1, 0:NBT], ones[0:NE, 0:1], amat[:], start=True, stop=True)
        M.matmul(zb[0][0:1, 0:NBT], nb[:], amat[:], start=True, stop=True).then_inc(S["cnt_filled"], 1)
        pe.wait_ge(S["tables_ready"], 1)
        nblk = pe.value_load(ctab[0:1, NE:NE + 1], min_val=EB, max_val=MAXB)

        def split_mm(o, pairs_, first=True, final=True):
            terms = [t for (xh_, xl_), (wh_, wl_) in pairs_ for t in ((xh_, wh_), (xh_, wl_), (xl_, wh_))]
            for n, (lhs, rhs) in enumerate(terms):
                last = M.matmul(o, lhs, rhs, start=(first and n == 0), stop=(final and n == len(terms) - 1))
            return last

        def unit(sl, u):
            return [t[:, ds(sl * UW + u, 1), :].rearrange("p s n -> p (s n)") for t in (wh, wl)]

        def gx(b, j, n):
            pe.wait_ge(S["gath"][j], n)
            for h in range(2):
                wait(pe, S["gx_lo"], 2 * b + h - 1)
                for kk in range(4):
                    k = 4 * h + kk
                    last = M.transpose(tp[h][:, kk * P:(kk + 1) * P], xg[j][:, k * P:(k + 1) * P], ident[:])
                last.then_inc(S["gx_filled"], 1)

        def buffer_of(b):
            return pe.value_load(btab[0:1, 2, ds(b, 1)], min_val=0, max_val=1) * -1 + 1

        def ordinal_of(b):
            return pe.value_load(btab[0:1, 1, ds(b, 1)], min_val=0, max_val=NE)

        def gate_up(b, j):
            sl, o = buffer_of(b), ordinal_of(b)
            pe.wait_ge(S["gx_lo"], 2 * b + 2)
            wait(pe, S["hh_ready"], b - 1)
            for k in range(0, KD, 2):
                pe.wait_ge(S["w_lo"], o * UW + k + 2)
                last = split_mm(zb[j][:], [((xh[:, i, :], xl[:, i, :]), unit(sl, i)) for i in (k, k + 1)], k == 0, k == KD - 2)
            last.then_inc(S["gu_filled"], 1)

        def down(b):
            sl, o = buffer_of(b), ordinal_of(b)
            pe.wait_ge(S["w_lo"], o * UW + UW)
            pe.wait_ge(S["ht_lo"], b + 1)
            wait(pe, S["o_act"], b)
            wait(pe, S["o_dve"], b)
            for n in range(2):
                last = split_mm(mx[n][:], [((hth[:, k, :], htl[:, k, :]), unit(sl, UG + 2 * k + n)) for k in range(KE)])
            last.then_inc(S["o_filled"], 1)

        def ht(b):
            pe.wait_ge(S["hh_ready"], b + 1)
            for k in range(KE):
                last = M.transpose(ly[:, k * P:(k + 1) * P], hh[:, k * P:(k + 1) * P], ident[:])
            last.then_inc(S["ht_filled"], 1)

        gx(0, 0, 16)
        gate_up(0, 0)
        gx(1, 1, 16)
        ht(0)

        def turn(q):
            for h in range(2):
                b, j = 2 * q + 1 + h, (1 + h) % 2
                gate_up(b, j)
                gx(b + 1, 1 - j, 16 * q + 32)
                down(b - 1)
                ht(b)

        turn(0)
        with pe.Fori(0, (MAXB - 1) // 2) as q:
            with pe.If(2 * q + 2 < nblk):
                turn(q + 1)
        turns = (nblk + 1) // 2
        pe.wait_ge(S["gath"][0], turns * 16 + 32)
        pe.wait_ge(S["gath"][1], turns * 16 + 16)
    ctx.close()


_INS = ["x_prompt", "x_sample", "state_pool", "state_conv", "c_prompt", "c_sample", "w_ada", "b_ada", "g_mix", "w_in",
        "w_pool", "pool_scale", "w_dw", "b_dw", "ln_g", "ln_b", "w_out", "g_ffn", "w_router", "b_router", "w_gate",
        "w_up", "w_down", "ws_gate", "ws_up", "ws_down", "w_ada_final", "b_ada_final", "g_final"]
_OUTS = [(1, SEQ, D), (NS, 1, D), (1, 1, POOLB, PW), (1, 1, CONVB, PW), (1, NS, POOLB, PW), (1, NS, CONVB, PW)]


def constants():
    import numpy as np

    f = np.float32
    t = np.arange(16)
    fix = np.stack([w / np.minimum(w, t + 1) for w in (2, 4, 8, 16)]).astype(f)
    b = np.arange(NBT)
    return {
        "ident": np.eye(P, dtype=f),
        "tri": np.triu(np.ones((P, P), f), 1),
        "ones": np.ones((P, P), f),
        "poolfix": np.ascontiguousarray(np.broadcast_to(fix, (P, CH, 16))),
        "iota64": np.ascontiguousarray(np.broadcast_to(np.arange(NE, dtype=f), (P, NE))),
        "base17": np.ascontiguousarray(np.broadcast_to(np.arange(NE, dtype=f) * EB, (P, NE))),
        "thr": np.ascontiguousarray(np.broadcast_to(np.array([-1.0] + [P * m for m in range(1, EB)], f), (NE, EB))),
        "uinc": np.triu(np.ones((NE, NE), f)),
        "brow": np.stack([np.where(b < EB, SHCOL + b, b - EB), b >= EB]).astype(f)[None],
        "biota": np.ascontiguousarray(np.broadcast_to(b.astype(f), (NE, NBT))),
    }


def kernel(**inputs):
    import numpy as np
    import concourse.bacc as bacc
    from concourse.bass_utils import run_bass_kernel_spmd as run

    nc = bacc.Bacc("TRN2", target_bir_lowering=False, num_devices=1)
    arrays, a, const = {}, {}, {}
    for name in _INS:
        arrays[f"in_{name}"] = np.ascontiguousarray(inputs[name])
        a[name] = nc.dram_tensor(f"in_{name}", arrays[f"in_{name}"].shape, F32, kind="ExternalInput").ap()
    for name, v in constants().items():
        arrays[f"const_{name}"] = v
        const[name] = nc.dram_tensor(f"const_{name}", v.shape, F32, kind="ExternalInput").ap()
    out = [nc.dram_tensor(f"out_{i}", s, F32, kind="ExternalOutput").ap() for i, s in enumerate(_OUTS)]
    program(nc, a, const, out)
    r = run(nc, [arrays], core_ids=[0])
    return tuple(r.results[0][f"out_{i}"] for i in range(len(_OUTS)))
```
